# Optimizing a Trainium2 kernel written in Bass

```python
import math
import jax, jax.numpy as jnp
from jax import lax
import numpy as np

D_MODEL = 1024
BATCH = 1
SEQ = 512
DEPTH = 2

CHUNK = 64
Q_BLOCK = 128
DSA_Q_BLOCK = 64
ROPE_THETA = 10000.0
HEAD_DIM = 64
LN_EPS = 1e-5
DIFF_HEADS = 4
DIFF_V_DIM = 2 * HEAD_DIM
DSA_HEADS = 8
IDX_HEADS = 4
DSA_TOPK_MAX = 256
IDX_W_SCALE = (IDX_HEADS * HEAD_DIM) ** -0.5
FOX_HEADS = 8
N_BRANCH = 3
BRANCH_WIDTH = 512
N_EXPERTS = 32
N_GROUPS = 4
EXPERTS_PER_GROUP = N_EXPERTS // N_GROUPS
TOP_K = 2
D_EXPERT = 512
MOE_BLOCK = 128
DEEPNORM_ALPHA = (2 * DEPTH) ** 0.25
DEEPNORM_BETA = (8 * DEPTH) ** -0.25
DIFF_QK_WIDTH = DIFF_HEADS * 2 * HEAD_DIM
DIFF_V_WIDTH = DIFF_HEADS * DIFF_V_DIM
DSA_WIDTH = DSA_HEADS * HEAD_DIM
IDX_Q_WIDTH = IDX_HEADS * HEAD_DIM
FOX_WIDTH = FOX_HEADS * HEAD_DIM
IN_SPLITS = (DIFF_QK_WIDTH, DIFF_QK_WIDTH, DIFF_V_WIDTH,
             DSA_WIDTH, DSA_WIDTH, DSA_WIDTH,
             IDX_Q_WIDTH, HEAD_DIM, IDX_HEADS,
             FOX_WIDTH, FOX_WIDTH, FOX_WIDTH, FOX_HEADS,
             N_BRANCH * D_MODEL)
IN_WIDTH = sum(IN_SPLITS)

kernel_name = 'hybrid_diff_dsa_fox_grouped_moe'

def layer_norm(x, g, b):
    xf = x.astype(jnp.float32)
    mu = jnp.mean(xf, axis=-1, keepdims=True)
    var = jnp.mean(jnp.square(xf - mu), axis=-1, keepdims=True)
    return ((xf - mu) * lax.rsqrt(var + LN_EPS) * g + b).astype(x.dtype)

def rms_norm(x, g):
    xf = x.astype(jnp.float32)
    y = xf * lax.rsqrt(jnp.mean(jnp.square(xf), axis=-1, keepdims=True) + LN_EPS)
    return (y * g).astype(x.dtype)

def rope_tables(positions, dim, dtype):
    inv = ROPE_THETA ** (-jnp.arange(0, dim, 2, dtype=jnp.float32) / dim)
    ang = positions.astype(jnp.float32)[..., None] * inv
    return jnp.cos(ang).astype(dtype), jnp.sin(ang).astype(dtype)

def apply_rope(x, cos, sin):
    shp = cos.shape[:2] + (1,) * (x.ndim - 3) + cos.shape[-1:]
    c, s = cos.reshape(shp), sin.reshape(shp)
    half = x.shape[-1] // 2
    x1, x2 = x[..., :half], x[..., half:]
    return jnp.concatenate([x1 * c - x2 * s, x2 * c + x1 * s], axis=-1)

def to_blocks(x, size):
    B, S = x.shape[:2]
    return jnp.moveaxis(x.reshape((B, S // size, size) + x.shape[2:]), 1, 0)

def from_blocks(x):
    x = jnp.moveaxis(x, 0, 1)
    return x.reshape((x.shape[0], x.shape[1] * x.shape[2]) + x.shape[3:])

def chunk_visible(qpos, kpos):
    return kpos[None, :] < (qpos[:, None] // CHUNK + 1) * CHUNK

def diff_attention(q, k, v, lam, norm_g, lam_init):
    B, S = q.shape[:2]
    nb = S // Q_BLOCK
    scale = HEAD_DIM ** -0.5
    kpos = jnp.arange(S)

    def block(args):
        qb, i = args
        vis = chunk_visible(i * Q_BLOCK + jnp.arange(Q_BLOCK), kpos)
        sc = jnp.einsum('bqhmd,bkhmd->bhmqk', qb, k).astype(jnp.float32) * scale
        p = jax.nn.softmax(jnp.where(vis, sc, -jnp.inf), axis=-1)
        a = p[:, :, 0] - lam * p[:, :, 1]
        return jnp.einsum('bhqk,bkhd->bqhd', a.astype(v.dtype), v)

    o = from_blocks(lax.map(block, (to_blocks(q, Q_BLOCK), jnp.arange(nb))))
    o = rms_norm(o, norm_g) * (1.0 - lam_init)
    return o.reshape(B, S, DIFF_V_WIDTH)

def dsa_attention(q, k, v, iq, ik, iw):
    B, S = q.shape[:2]
    topk = min(DSA_TOPK_MAX, S // 4)
    nb = S // DSA_Q_BLOCK
    scale = HEAD_DIM ** -0.5
    kpos = jnp.arange(S)
    gather = jax.vmap(lambda t, idx: t[idx])

    def block(args):
        qb, iqb, iwb, i = args
        vis = chunk_visible(i * DSA_Q_BLOCK + jnp.arange(DSA_Q_BLOCK), kpos)
        logits = jnp.einsum('bqhd,bkd->bqhk', iqb, ik).astype(jnp.float32)
        score = jnp.einsum('bqh,bqhk->bqk', iwb.astype(jnp.float32), jax.nn.relu(logits))
        score = jnp.where(vis, score, -jnp.inf)
        top_val, top_idx = lax.top_k(score, topk)
        valid = jnp.isfinite(top_val)
        kg = gather(k, top_idx)
        vg = gather(v, top_idx)
        sc = jnp.einsum('bqhd,bqkhd->bhqk', qb, kg).astype(jnp.float32) * scale
        p = jax.nn.softmax(jnp.where(valid[:, None], sc, -jnp.inf), axis=-1)
        return jnp.einsum('bhqk,bqkhd->bqhd', p.astype(v.dtype), vg)

    o = lax.map(block, (to_blocks(q, DSA_Q_BLOCK), to_blocks(iq, DSA_Q_BLOCK),
                        to_blocks(iw, DSA_Q_BLOCK), jnp.arange(nb)))
    return from_blocks(o).reshape(B, S, DSA_WIDTH)

def forgetting_attention(q, k, v, log_f):
    B, S = q.shape[:2]
    nb = S // Q_BLOCK
    scale = HEAD_DIM ** -0.5
    kpos = jnp.arange(S)
    c = lax.cumsum(log_f, axis=1)
    cT = jnp.transpose(c, (0, 2, 1))

    def block(args):
        qb, cqb, i = args
        qpos = i * Q_BLOCK + jnp.arange(Q_BLOCK)
        causal = kpos[None, :] <= qpos[:, None]
        sc = jnp.einsum('bqhd,bkhd->bhqk', qb, k).astype(jnp.float32) * scale
        sc = sc + jnp.transpose(cqb, (0, 2, 1))[..., None] - cT[:, :, None, :]
        p = jax.nn.softmax(jnp.where(causal, sc, -jnp.inf), axis=-1)
        return jnp.einsum('bhqk,bkhd->bqhd', p.astype(v.dtype), v)

    o = lax.map(block, (to_blocks(q, Q_BLOCK), to_blocks(c, Q_BLOCK), jnp.arange(nb)))
    return from_blocks(o).reshape(B, S, FOX_WIDTH)

def hybrid_mixer(x, cos, sin, w_in, b_forget, diff_lam, diff_norm_g, w_br, w_o, lam_init):
    B, S, D = x.shape
    z = x @ w_in
    split_at = np.cumsum(IN_SPLITS)[:-1].tolist()
    dq, dk, dv, sq, sk, sv, iq, ik, iw, fq, fk, fv, ff, g = jnp.split(z, split_at, axis=-1)

    dq = apply_rope(dq.reshape(B, S, DIFF_HEADS, 2, HEAD_DIM), cos, sin)
    dk = apply_rope(dk.reshape(B, S, DIFF_HEADS, 2, HEAD_DIM), cos, sin)
    lamf = diff_lam.astype(jnp.float32)
    lam = (jnp.exp(jnp.sum(lamf[0] * lamf[1])) - jnp.exp(jnp.sum(lamf[2] * lamf[3]))
           + lam_init)
    o_diff = diff_attention(dq, dk, dv.reshape(B, S, DIFF_HEADS, DIFF_V_DIM),
                            lam, diff_norm_g, lam_init)

    sq = apply_rope(sq.reshape(B, S, DSA_HEADS, HEAD_DIM), cos, sin)
    sk = apply_rope(sk.reshape(B, S, DSA_HEADS, HEAD_DIM), cos, sin)
    iq = apply_rope(iq.reshape(B, S, IDX_HEADS, HEAD_DIM), cos, sin)
    ik = apply_rope(ik, cos, sin)
    o_dsa = dsa_attention(sq, sk, sv.reshape(B, S, DSA_HEADS, HEAD_DIM),
                          iq, ik, iw * IDX_W_SCALE)

    log_f = jax.nn.log_sigmoid(ff.astype(jnp.float32) + b_forget)
    o_fox = forgetting_attention(fq.reshape(B, S, FOX_HEADS, HEAD_DIM),
                                 fk.reshape(B, S, FOX_HEADS, HEAD_DIM),
                                 fv.reshape(B, S, FOX_HEADS, HEAD_DIM), log_f)

    gates = jax.nn.sigmoid(g.astype(jnp.float32)).astype(x.dtype).reshape(B, S, N_BRANCH, D)
    y = (gates[:, :, 0] * (o_diff @ w_br[0])
         + gates[:, :, 1] * (o_dsa @ w_br[1])
         + gates[:, :, 2] * (o_fox @ w_br[2]))
    return y @ w_o

def grouped_moe(x, w_router, b_router, w_gate, w_up, w_down):
    B, S, D = x.shape
    T = B * S
    A = T * TOP_K
    xt = x.reshape(T, D)
    aff = jax.nn.sigmoid((xt @ w_router).astype(jnp.float32))
    sel = (aff + b_router.astype(jnp.float32)).reshape(T, N_GROUPS, EXPERTS_PER_GROUP)
    grp_score = jnp.sum(lax.top_k(sel, 2)[0], axis=-1)
    g_idx = jnp.argmax(grp_score, axis=-1).astype(jnp.int32)
    in_grp = jnp.take_along_axis(sel, g_idx[:, None, None], axis=1)[:, 0]
    _, loc = lax.top_k(in_grp, TOP_K)
    e_idx = g_idx[:, None] * EXPERTS_PER_GROUP + loc
    wts = jnp.take_along_axis(aff, e_idx, axis=1)
    wts = wts / jnp.sum(wts, axis=-1, keepdims=True)

    flat_e = e_idx.reshape(A)
    order = jnp.argsort(flat_e)
    e_sorted = flat_e[order]
    tok_sorted = order // TOP_K
    w_sorted = wts.reshape(A)[order]
    counts = jnp.bincount(flat_e, length=N_EXPERTS)
    padded = (counts + MOE_BLOCK - 1) // MOE_BLOCK * MOE_BLOCK
    pad_end = jnp.cumsum(padded)
    pad_start = pad_end - padded
    start = jnp.cumsum(counts) - counts
    dest = pad_start[e_sorted] + jnp.arange(A) - start[e_sorted]
    R = -(-A // MOE_BLOCK) * MOE_BLOCK + N_EXPERTS * MOE_BLOCK
    nblk = R // MOE_BLOCK
    row_tok = jnp.full((R,), T, dtype=tok_sorted.dtype).at[dest].set(tok_sorted)
    x_rows = jnp.concatenate([xt, jnp.zeros((1, D), xt.dtype)], axis=0)[row_tok]
    x_rows = x_rows.reshape(nblk, MOE_BLOCK, D)
    blk_e = jnp.minimum(jnp.searchsorted(pad_end, jnp.arange(nblk) * MOE_BLOCK, side='right'),
                        N_EXPERTS - 1)

    def expert_block(args):
        xb, e = args
        h = jax.nn.silu(xb @ w_gate[e]) * (xb @ w_up[e])
        return h @ w_down[e]

    y_rows = lax.map(expert_block, (x_rows, blk_e)).reshape(R, D)
    y = y_rows[dest] * w_sorted[:, None].astype(x.dtype)
    return jnp.zeros((T, D), x.dtype).at[tok_sorted].add(y).reshape(B, S, D)

def setup_inputs(seed: int = 0) -> dict:
    key = jax.random.key(seed)
    ks = jax.random.split(key, 20)

    def nrm(k, shape, scale):
        return jax.random.normal(k, shape, jnp.float32) * scale

    x = nrm(ks[0], (BATCH, SEQ, D_MODEL), 1.0)
    offset = jax.random.randint(ks[1], (BATCH, 1), 0, SEQ, dtype=jnp.int32)
    positions = offset + jnp.arange(SEQ, dtype=jnp.int32)[None, :]
    return {
        'x': x,
        'positions': positions,
        'ln_in_g': 1.0 + nrm(ks[2], (D_MODEL,), 0.02),
        'ln_in_b': nrm(ks[3], (D_MODEL,), 0.02),
        'w_in': nrm(ks[4], (DEPTH, D_MODEL, IN_WIDTH), D_MODEL ** -0.5),
        'b_forget': 3.0 + nrm(ks[5], (DEPTH, FOX_HEADS), 0.5),
        'diff_lam': nrm(ks[6], (DEPTH, 4, HEAD_DIM), 0.1),
        'diff_norm_g': 1.0 + nrm(ks[7], (DEPTH, DIFF_V_DIM), 0.02),
        'w_br': nrm(ks[8], (DEPTH, N_BRANCH, BRANCH_WIDTH, D_MODEL),
                    BRANCH_WIDTH ** -0.5 * DEEPNORM_BETA),
        'w_o': nrm(ks[9], (DEPTH, D_MODEL, D_MODEL), D_MODEL ** -0.5 * DEEPNORM_BETA),
        'ln1_g': 1.0 + nrm(ks[10], (DEPTH, D_MODEL), 0.02),
        'ln1_b': nrm(ks[11], (DEPTH, D_MODEL), 0.02),
        'w_router': nrm(ks[12], (D_MODEL, N_EXPERTS), D_MODEL ** -0.5),
        'b_router': nrm(ks[13], (N_EXPERTS,), 0.01),
        'w_gate': nrm(ks[14], (DEPTH, N_EXPERTS, D_MODEL, D_EXPERT), D_MODEL ** -0.5),
        'w_up': nrm(ks[15], (DEPTH, N_EXPERTS, D_MODEL, D_EXPERT), D_MODEL ** -0.5),
        'w_down': nrm(ks[16], (DEPTH, N_EXPERTS, D_EXPERT, D_MODEL),
                      D_EXPERT ** -0.5 * DEEPNORM_BETA),
        'ln2_g': 1.0 + nrm(ks[17], (DEPTH, D_MODEL), 0.02),
        'ln2_b': nrm(ks[18], (DEPTH, D_MODEL), 0.02),
    }

def reference(x, positions, ln_in_g, ln_in_b, w_in, b_forget, diff_lam, diff_norm_g,
              w_br, w_o, ln1_g, ln1_b, w_router, b_router, w_gate, w_up, w_down,
              ln2_g, ln2_b):
    cos, sin = rope_tables(positions, HEAD_DIM, x.dtype)
    h = layer_norm(x, ln_in_g, ln_in_b)
    for l in range(DEPTH):
        lam_init = 0.8 - 0.6 * math.exp(-0.3 * l)
        m = hybrid_mixer(h, cos, sin, w_in[l], b_forget[l], diff_lam[l], diff_norm_g[l],
                         w_br[l], w_o[l], lam_init)
        h = layer_norm(DEEPNORM_ALPHA * h + m, ln1_g[l], ln1_b[l])
        f = grouped_moe(h, w_router, b_router, w_gate[l], w_up[l], w_down[l])
        h = layer_norm(DEEPNORM_ALPHA * h + f, ln2_g[l], ln2_b[l])
    return h


_drawn_inputs = setup_inputs


def setup_inputs(seed=0):
    import zlib

    import numpy as np

    out = dict(_drawn_inputs(seed))
    spreads = {}
    factors = {'diff_norm_g': 3.552}
    for name, (base, spread) in spreads.items():
        noise = np.random.default_rng([zlib.crc32(name.encode()), seed]).standard_normal(out[name].shape)
        drawn = base * np.exp(spread * noise) if base else spread * noise
        out[name] = __import__('jax').numpy.asarray(drawn.astype(out[name].dtype))
    for name, factor in factors.items():
        out[name] = (out[name] * factor).astype(out[name].dtype)
    return out
```

```python
import math
from contextlib import ExitStack

import numpy as np
import concourse.bass as bass
from concourse import mybir

ALU = mybir.AluOpType
ACT = mybir.ActivationFunctionType
AX = mybir.AxisListType
F32 = mybir.dt.float32
BF16 = mybir.dt.bfloat16
I32 = mybir.dt.int32
U32 = mybir.dt.uint32

P = 128
T = 512
NT = T // P
D = 1024
KD = D // P
DEPTH = 2
HD = 64
CHUNK = 64
EPS = 1e-5
ALPHA = (2 * DEPTH) ** 0.25
SCALE = HD ** -0.5
NEG = -1e30
TAKEN = -3e38
TOPK = 128
NEXP = 32
NGRP = 4
EPG = NEXP // NGRP
DE = 512
FE = DE // P
BW = 512
KB = BW // P
IDX_H = 4
W_IN = 8012
COL = dict(dq=0, dk=512, dv=1024, sq=1536, sk=2048, sv=2560, iq=3072, ik=3328, iw=3392,
           fq=3396, fk=3908, fv=4420, ff=4932, g=4940)
BRANCHES = ("f", "d", "s")
WBR = dict(d=0, s=1, f=2)
PAIRS = 4
NSTEP = PAIRS * NT

CAP = 80
NOV = (2 * T - 1) // CAP
OVQ = (T - 1) // CAP
NBLK = NEXP + NOV
NPAIR = NEXP // 2
RING = 6
PIECE = 4096

MAGIC = 12582912.0
PI_LO = 3.1415925
C1, C2 = 6.28125, 0.0019350051879882812
C3 = 2 * math.pi - C1 - C2


class Signal:

    def __init__(self, book, name, sem, turns=NPAIR):
        self.book, self.sem, self.turns = book, sem, turns
        self.total = book.totals.setdefault(name, dict(pre=0, layer=0, pair=0, tail=0, post=0, over=0))
        self.marks = book.marks.setdefault(name, {})
        self.n = dict.fromkeys(self.total, 0)
        book.live[name] = self.n

    def tick(self, key=None, by=1):
        s = self.book.scope
        self.n[s] += by
        if key is not None:
            self.marks[key] = (s, self.n[s])
        return by

    def value(self, s, n, l, i):
        c = self.total
        layer = c["layer"] + self.turns * c["pair"] + c["tail"]
        if s == "pre":
            return n
        if s == "over":
            return i * c["over"] + (c["pre"] + n)
        if s == "layer":
            return l * layer + (c["pre"] + n)
        if s == "pair":
            return l * layer + i * c["pair"] + (c["pre"] + c["layer"] + n)
        if s == "tail":
            return l * layer + (c["pre"] + c["layer"] + self.turns * c["pair"] + n)
        return c["pre"] + DEPTH * layer + n

    def at(self, key, l=0, i=NPAIR - 1):
        s, n = self.marks.get(key, ("pre", 0))
        return self.value(s, n, l, i)

    def start(self, l=0, i=0):
        return self.value(self.book.scope if self.book.scope == "pair" else "layer", 0, l, i)

    def now(self, l=0, i=NPAIR - 1):
        return self.value(self.book.scope, self.n[self.book.scope], l, i)


class Book:
    def __init__(self):
        self.totals, self.marks, self.live, self.where, self.scope = {}, {}, {}, {}, "pre"

    def close(self):
        same = self.totals == self.live
        self.totals, self.live = {k: dict(v) for k, v in self.live.items()}, {}
        return same


class Bank:
    def __init__(self, book, b, tensor, full, read):
        self.t = tensor
        self.full = Signal(book, f"bank{b}", full)
        self.read = read


def trunk(nc, book, ins, out):
    (x, positions, ln_in_g, ln_in_b, w_in, b_forget, diff_lam, diff_norm_g, w_br, w_o, ln1_g, ln1_b,
     w_router, b_router, w_gate, w_up, w_down, ln2_g, ln2_b,
     c_f32, c_bf16, c_lam) = ins
    C = CAP
    x_rows = nc.dram_tensor("x_rows", [NBLK * C, D], F32).ap()
    y_rows = nc.dram_tensor("y_rows", [NBLK * C, D], F32).ap()

    with ExitStack() as ctx:
        def sb(name, shape, dt=F32):
            return ctx.enter_context(nc.sbuf_tensor(name, shape, dt))

        def signal(name, turns=NPAIR):
            return Signal(book, name, ctx.enter_context(nc.semaphore(name)), turns)

        ps = ctx.enter_context(nc.psum_tensor("ps", [P, 8, 512], F32))
        bank = [Bank(book, b, ps[:, b, :], ctx.enter_context(nc.semaphore(f"bank{b}_full")),
                     ctx.enter_context(nc.semaphore(f"bank{b}_read"))) for b in range(8)]

        h = sb("h", [P, NT, D])
        hT = sb("hT", [P, KD, T])
        ring = sb("ring", [P, RING, PIECE])
        cf = sb("cf", [P, 4 * P + NEXP * 2 + 3 + 8])
        cb = sb("cb", [P, 3 * P], BF16)
        ident, perm, tri, ones = (cf[:, i * P:(i + 1) * P] for i in range(4))
        iota_e = cf[:, 4 * P:4 * P + NEXP]
        iota_g = cf[:, 4 * P + NEXP:4 * P + 2 * NEXP]
        c0 = 4 * P + 2 * NEXP
        inv_freq, sign_half, m_half = cf[:, c0:c0 + 1], cf[:, c0 + 1:c0 + 2], cf[:, c0 + 2:c0 + 3]
        pick = cf[0:8, c0 + 3:c0 + 11]
        identb, chunk_mask, causal_mask = (cb[:, i * P:(i + 1) * P] for i in range(3))
        zeros = sb("zeros", [P, NEXP])
        wr = sb("wr", [P, KD, NEXP])
        br = sb("br", [P, NEXP])
        w_ff = sb("w_ff", [P, KD, 8])
        b_f = sb("b_f", [8, 1])
        lamv = sb("lamv", [P, 4, HD])
        lamw = sb("lamw", [P, 8])
        laminit = sb("laminit", [P, 2])
        norm_g = sb("norm_g", [P, P])
        iw = sb("iw", [P, NT, IDX_H])
        small = sb("small", [P, 64])
        stats = sb("stats", [P, NT, 2, 6])
        moments = sb("moments", [P, NT, 2])
        rstd = sb("rstd", [P, NT])

        scr = sb("scr", [P, 18176])
        qT = scr[:, 0:2048].rearrange("p (b t) -> p b t", t=T)
        kT = scr[:, 2048:4096].rearrange("p (b t) -> p b t", t=T)
        v = scr[:, 4096:6144].rearrange("p (b t) -> p b t", t=T)
        yT = scr[:, 6144:10240].rearrange("p (b t) -> p b t", t=T)
        iqT = scr[:, 6144:7168].rearrange("p (b t) -> p b t", t=T)
        ikT = scr[:, 7168:7680]
        oT = scr[:, 10240:12288].rearrange("p (b t) -> p b t", t=T)
        pbuf = scr[:, 12288:14336].rearrange("p (n j k) -> p n j k", n=2, j=2)
        z = [scr[:, 12288:12800], scr[:, 12800:13312]]
        r1, r2 = scr[:, 13312:13824], scr[:, 13824:14336]
        gate = [scr[:, 12288:12800], scr[:, 12800:13312]]
        prod = scr[:, 13312:13824]
        ptb = scr[:, 14336:16384].rearrange("p (n w) -> p n w", n=2)
        relu = [scr[:, 14336:14848], scr[:, 14848:15360]]
        ffx, ffe = scr[0:8, 15360:15872], scr[0:8, 15872:16384]
        score = {1: scr[:, 10240:10496], 2: scr[:, 10496:10880], 3: scr[:, 10880:11392]}
        zero_row = scr[:, 8192:9216]
        cT = scr[0:8, 9728:10240]
        keep = scr[:, 16384:17152].bitcast(BF16)
        cos, sin = scr[:, 17152:17664], scr[:, 17664:18176]
        onorm = [sb("onorm0", [P, P])[:, :], sb("onorm1", [P, P])[:, :]]
        ln_g, ln_b = scr[:, 4096:5120], scr[:, 5120:6144]
        xin = [scr[0:C, 0:1024], scr[0:C, 1024:2048]]
        ysb = [scr[0:C, 2048:3072], scr[0:C, 3072:4096]]
        got = [[scr[:, 6144 + (2 * n + k) * 1024:6144 + (2 * n + k + 1) * 1024] for k in range(2)] for n in range(2)]
        xT = [scr[:, 10240 + n * KD * C:10240 + (n + 1) * KD * C].rearrange("p (k c) -> p k c", c=C) for n in range(2)]
        hid = [scr[:, 11520 + n * 384:11520 + n * 384 + FE * C].rearrange("p (k c) -> p k c", c=C) for n in range(2)]
        act_g = [scr[:, 12288 + n * 512:12288 + n * 512 + FE * C].rearrange("p (k c) -> p k c", c=C) for n in range(2)]
        RT = 14336
        aff = scr[:, RT:RT + 128].rearrange("p (t e) -> p t e", e=NEXP)
        sel = scr[:, RT + 128:RT + 256].rearrange("p (t e) -> p t e", e=NEXP)
        srt = scr[:, RT + 256:RT + 384].rearrange("p (g e) -> p g e", e=EPG)
        gsc = scr[:, RT + 384:RT + 416].rearrange("p (t g) -> p t g", g=8)
        gtop = scr[:, RT + 416:RT + 448].rearrange("p (t g) -> p t g", g=8)
        gidx = scr[:, RT + 448:RT + 480].bitcast(U32).rearrange("p (t g) -> p t g", g=8)
        gidf = scr[:, RT + 480:RT + 484]
        etop = scr[:, RT + 484:RT + 516].rearrange("p (t g) -> p t g", g=8)
        eidx = scr[:, RT + 516:RT + 548].bitcast(U32).rearrange("p (t g) -> p t g", g=8)
        eidf = scr[:, RT + 548:RT + 556].rearrange("p (k t) -> p k t", k=2)
        hot = scr[:, RT + 560:RT + 816].rearrange("p (k t e) -> p k t e", k=2, e=NEXP)
        both = scr[:, RT + 816:RT + 944].rearrange("p (t e) -> p t e", e=NEXP)
        gm = scr[:, RT + 944:RT + 1072].rearrange("p (t e) -> p t e", e=NEXP)
        tmp = scr[:, RT + 1072:RT + 1200].rearrange("p (t e) -> p t e", e=NEXP)
        cum = scr[:, RT + 1200:RT + 1232]
        ovc = scr[:, RT + 1232:RT + 1264]
        base = scr[:, RT + 1264:RT + 1296]
        k8 = [scr[:, RT + 1296 + 8 * i:RT + 1304 + 8 * i].rearrange("p (k t) -> p k t", k=2) for i in range(8)]
        wts, rank, quo, bas, slotf, r8a, r8b, wsum = k8
        slot = scr[:, RT + 1360:RT + 1368].bitcast(U32).rearrange("p (k t) -> p k t", k=2)
        ovt = scr[0:1, RT + 1368:RT + 1368 + NOV * NEXP].rearrange("p (j e) -> p j e", e=NEXP)
        schedf = scr[0:1, RT + 1368 + NOV * NEXP:RT + 1368 + NOV * NEXP + 1 + NOV]
        wts_keep = sb("wts_keep", [P, 2, NT])
        slot_keep = sb("slot_keep", [P, 2, NT], U32)
        sched = sb("sched", [1, 1 + NOV], I32)
        neg_max = [small[:, 0:2], small[:, 2:4]]
        psum_row = [small[:, 4:6], small[:, 6:8]]
        rcp = [small[:, 8:10], small[:, 10:12]]
        rcl = [small[:, 12:13], small[:, 13:14]]
        ssq = [small[:, 14:15], small[:, 15:16]]
        rms = [small[:, 16:17], small[:, 17:18]]
        rms_t = [small[:, 18:19], small[:, 19:20]]
        top8 = small[:, 24:32]
        lameps = small[:, 32:36]
        neg_lam = lamw[:, 0:1]
        gscale = lamw[:, 1:2]

        const_land = signal("const_land")
        idle = ctx.enter_context(nc.semaphore("idle"))
        x_land = signal("x_land")
        pos_land = signal("pos_land")
        zero_land = signal("zero_land")
        small_land = signal("small_land")
        ln_land = signal("ln_land")
        out_land = signal("out_land")
        land = [signal(f"land{s}", NPAIR - 1) for s in range(RING)]
        dve_seq = signal("dve_seq")
        act_seq = signal("act_seq")
        pool_seq = signal("pool_seq")
        moments_ready = signal("moments_ready")
        rstd_ready = signal("rstd_ready")
        h_ready = signal("h_ready")
        angle_ready = signal("angle_ready")
        roped = signal("roped")
        ffe_ready = signal("ffe_ready")
        ffl_ready = signal("ffl_ready")
        lam_prod = signal("lam_prod")
        lam_exp = signal("lam_exp")
        cum_ready = signal("cum_ready")
        keep_ready = signal("keep_ready")
        max_ready = signal("max_ready")
        p_ready = signal("p_ready")
        ssq_ready = signal("ssq_ready")
        rms_ready = signal("rms_ready")
        y_ready = signal("y_ready")
        aff_ready = signal("aff_ready")
        hot_ready = signal("hot_ready")
        slot_ready = signal("slot_ready")
        scattered = signal("scattered")
        xin_land = [signal(f"xin_land{n}") for n in range(2)]
        y_stored = [signal(f"y_stored{n}") for n in range(2)]
        ysb_free = [signal(f"ysb_free{n}") for n in range(2)]
        got_land = [signal(f"got_land{n}") for n in range(2)]
        got_used = signal("got_used")
        sched_ready = signal("sched_ready")
        over_w = signal("over_w")
        over_x = signal("over_x")
        over_t = signal("over_t")
        over_xT = signal("over_xT")
        over_gu = signal("over_gu")
        over_act = signal("over_act")
        over_h = signal("over_h")
        over_y = signal("over_y")
        over_ye = signal("over_ye")
        over_st = signal("over_st")

        pieces = ["idx"]
        for b in BRANCHES:
            pieces += [b + "q", b + "k", b + "v", b + "g0", b + "g1", b + "br"]
        pieces += ["wo0", "wo1"]
        in_slot = {name: n % RING for n, name in enumerate(pieces)}

        def cols(slot, k0=KD):
            return ring[:, slot, :].rearrange("p (k c) -> p k c", k=k0)

        idx_cols = ring[:, in_slot["idx"], 0:KD * 388].rearrange("p (k c) -> p k c", c=388)

        last_reader = {"idx": "ik", "wo0": ("m", NT - 1, 1), "wo1": ("m", NT - 1, 1)}
        for b in BRANCHES:
            last_reader |= {b + "q": (b + "q", KB - 1), b + "k": (b + "k", KB - 1), b + "v": (b + "v", NT - 1),
                            b + "g0": ("g", b, 3), b + "g1": ("g", b, KD - 1), b + "br": ("br", b, KD - 1)}

        def width(t):
            return (t + 1) * P

        def tok(t):
            return slice(t * P, (t + 1) * P)

        with nc.Block() as block:

            def over_load(sp, one, j, b):
                sp.wait_ge(over_y.sem, over_y.value("over", 0, 0, b))
                alone(sp)
                e = sp.value_load(sched[0:1, bass.ds(j + 1, 1)], min_val=0, max_val=NEXP - 1)
                for s, w in enumerate((w_gate, w_up, w_down)):
                    src = w[one, bass.ds(e, 1)].rearrange("o q (k p) c -> p (o q k) c", p=P)
                    sp.dma_start(cols(s, FE if s == 2 else KD), src).then_inc(over_w.sem, over_w.tick(by=16))
                sp.wait_ge(over_y.sem, over_y.value("over", 1, 0, b))
                alone(sp)

            def alone(eng):
                eng.sem_inc(idle, 1)

            blocks_before = {}

            def count_blocks(eng):
                blocks_before[eng.engine] = eng.alloc_register("blocks_before_" + eng.engine.name)
                eng.reg_mov(blocks_before[eng.engine], 0)

            def overflow(eng, l, body):
                eng.wait_ge(sched_ready.sem, sched_ready.at("sched", l))
                alone(eng)
                n_over = eng.value_load(sched[0:1, 0:1], min_val=0, max_val=NOV)
                before = eng.snap(blocks_before[eng.engine], min_val=0, max_val=NOV * DEPTH)
                with eng.Fori(0, NOV) as j:
                    with eng.If(j < n_over):
                        book.scope = "over"
                        body(j, before + j)
                book.scope = "tail"
                eng.reg_add(blocks_before[eng.engine], blocks_before[eng.engine], n_over)

            @block.sync
            def _(sp):
                book.scope = "pre"
                sp.dma_start(h[:, :, :], x[0].rearrange("(t p) d -> p t d", p=P)).then_inc(
                    x_land.sem, x_land.tick("all", 16))
                for src, dst in ((c_f32, cf[:, :]), (c_bf16, cb[:, :]),
                                 (w_router.rearrange("(k p) e -> p k e", p=P), wr[:, :, :]),
                                 (b_router.partition_broadcast(P), br[:, :]),
                                 (ln_in_g.partition_broadcast(P), ln_g),
                                 (ln_in_b.partition_broadcast(P), ln_b)):
                    sp.dma_start(dst, src).then_inc(const_land.sem, const_land.tick("all", 16))
                sp.dma_start(r1.bitcast(I32), positions[0].partition_broadcast(P)).then_inc(
                    pos_land.sem, pos_land.tick("all", 16))

                count_blocks(sp)
                with sp.Fori(0, DEPTH) as l:
                    book.scope = "layer"
                    one = bass.ds(l, 1)

                    def multiplied(key, i=NPAIR - 1):
                        b = book.where.get(key, 0)
                        sp.wait_ge(bank[b].full.sem, bank[b].full.at(key, l, i))
                        alone(sp)

                    for n, name in enumerate(pieces):
                        s = in_slot[name]
                        if n == RING:
                            sp.wait_ge(h_ready.sem, h_ready.start(l))
                            alone(sp)
                            for src, dst in (
                                    (w_in[one, :, COL["ff"]:COL["ff"] + 8].rearrange("o (k p) c -> p (o k) c", p=P), w_ff[:, :, :]),
                                    (b_forget[one, :].rearrange("o c -> c o"), b_f[:, :]),
                                    (diff_lam[one].rearrange("o a d -> (o a d)").partition_broadcast(P),
                                     lamv[:, :, :].rearrange("p a d -> p (a d)")),
                                    (c_lam[one, :].rearrange("o c -> (o c)").partition_broadcast(P), laminit[:, :]),
                                    (diff_norm_g[one, :].rearrange("o c -> (o c)").partition_broadcast(P), norm_g[:, :])):
                                sp.dma_start(dst, src).then_inc(small_land.sem, small_land.tick("all", 16))
                        if n >= RING:
                            multiplied(last_reader[pieces[n - RING]])
                        if name == "idx":
                            parts = [(w_in[one, :, COL["iq"]:COL["iw"]].rearrange("o (k p) c -> p (o k) c", p=P),
                                      idx_cols[:, :, 0:320]),
                                     (w_in[one, :, COL["ik"]:COL["fq"]].rearrange("o (k p) c -> p (o k) c", p=P),
                                      idx_cols[:, :, 320:388])]
                        elif name[1:] == "br":
                            parts = [(w_br[one, WBR[name[0]]].rearrange("o (k p) c -> p (o k) c", p=P), cols(s, KB))]
                        elif name[:2] == "wo":
                            r0 = int(name[2]) * BW
                            parts = [(w_o[one, r0:r0 + BW, :].rearrange("o (k p) c -> p (o k) c", p=P), cols(s, KB))]
                        else:
                            c = COL[name] if name in COL else COL["g"] + WBR[name[0]] * D + int(name[2]) * BW
                            parts = [(w_in[one, :, c:c + BW].rearrange("o (k p) c -> p (o k) c", p=P), cols(s))]
                        for src, dst in parts:
                            sp.dma_start(dst, src).then_inc(land[s].sem, land[s].tick(name, 16))

                    def expert_piece(n, m, e, key):
                        s = 3 * n + m
                        src = (w_gate, w_up, w_down)[m][one, e].rearrange("o q (k p) c -> p (o q k) c", p=P)
                        sp.dma_start(cols(s, FE if m == 2 else KD), src).then_inc(land[s].sem, land[s].tick(key, 16))

                    for s in (3, 4, 5, 0, 1, 2):
                        multiplied(last_reader[[p_ for p_ in pieces if in_slot[p_] == s][-1]])
                        expert_piece(s // 3, s % 3, slice(s // 3, s // 3 + 1), ("first", s))
                    with sp.Fori(0, NPAIR - 1) as i:
                        book.scope = "pair"
                        for n in range(2):
                            for m in range(3):
                                multiplied(("y", n, 1) if m == 2 else ("gu", n, m), i)
                                expert_piece(n, m, bass.ds(i * 2 + 2 + n, 1), None)
                    book.scope = "tail"
                    multiplied(("y", 1, 1))
                    overflow(sp, l, lambda j, b: over_load(sp, one, j, b))

            @block.tensor
            def _(pe):
                mm = nc.tensor.matmul
                turn = {"pj": 0, "rope": 0}
                rope_src = {}

                def free(b, l=0, i=0):
                    pe.wait_ge(bank[b].read, bank[b].full.now(l, i))

                def filled(ins, b, key):
                    book.where[key] = b
                    ins.then_inc(bank[b].full.sem, bank[b].full.tick(key))

                def in_sbuf(b, key, l=0, i=NPAIR - 1):
                    pe.wait_ge(bank[b].read, bank[b].full.at(key, l, i))

                def transpose_tile(key, t, l=0):
                    pe.wait_ge(h_ready.sem, h_ready.at((key, t), l))
                    for half in range(2):
                        b = 2 * (t % 2) + half
                        free(b, l)
                        for k in range(4):
                            kd = 4 * half + k
                            ins = nc.tensor.transpose(bank[b].t[:, k * P:(k + 1) * P],
                                                      h[:, t, kd * P:(kd + 1) * P], ident)
                        filled(ins, b, (key, t, half))

                def transpose_h(key, l=0):
                    for t in range(NT):
                        transpose_tile(key, t, l)

                def project(key, l, weights, M=P):
                    b = turn["pj"] % 4
                    turn["pj"] += 1
                    free(b, l)
                    for k in range(KD):
                        ins = mm(bank[b].t[0:M, :], weights(k), hT[:, k, :], start=(k == 0), stop=(k == KD - 1))
                    filled(ins, b, key)
                    return ins

                def turn_halves(l, r):
                    b = 4 + r % 2
                    zb, zkey = rope_src[r]
                    in_sbuf(zb, zkey, l)
                    free(b, l)
                    filled(mm(bank[b].t, perm, z[r % 2], start=True, stop=True), b, ("rope", r))

                def roped_blocks(keys, l, weights, name=None):
                    for n, key in enumerate(keys):
                        project(key, l, lambda k: weights(n, k))
                        r = turn["rope"]
                        turn["rope"] += 1
                        rope_src[r] = (book.where[key], key)
                        if n:
                            turn_halves(l, r - 1)
                    turn_halves(l, turn["rope"] - 1)

                def landed(name, l):
                    s = in_slot[name]
                    pe.wait_ge(land[s].sem, land[s].at(name, l))

                def index_logits(l):
                    landed("idx", l)
                    b = turn["pj"] % 4
                    turn["pj"] += 1
                    free(b, l)
                    for t in range(NT):
                        for k in range(KD):
                            ins = mm(bank[b].t[:, t * IDX_H:(t + 1) * IDX_H], hT[:, k, tok(t)],
                                     idx_cols[:, k, 384:388], start=(k == 0), stop=(k == KD - 1))
                    filled(ins, b, "iw")
                    roped_blocks(["iq0", "iq1", "ik"], l, lambda n, k: idx_cols[:, k, n * P:(n + 1) * P])
                    pe.wait_ge(roped.sem, roped.at("ik", l))
                    for t in range(1, NT):
                        for hd in range(IDX_H):
                            free(hd, l)
                            rows = slice(HD * (hd % 2), HD * (hd % 2) + HD)
                            ins = mm(bank[hd].t[:, 0:width(t)], iqT[rows, hd // 2, tok(t)],
                                     ikT[rows, 0:width(t)], start=True, stop=True)
                            filled(ins, hd, ("logit", t, hd))
                    turn["pj"] = 0

                def forget_logits(l):
                    pe.wait_ge(small_land.sem, small_land.at("all", l))
                    project("ff", l, lambda k: w_ff[:, k, :], M=8)

                def queries_keys_values(br, l):
                    for what in "qk":
                        name = br + what
                        landed(name, l)
                        w = cols(in_slot[name])
                        if br == "f":
                            for n in range(KB):
                                ins = project((name, n), l, lambda k: w[:, k, n * P:(n + 1) * P])
                        else:
                            roped_blocks([(name, n) for n in range(KB)], l, lambda n, k: w[:, k, n * P:(n + 1) * P])
                    name = br + "v"
                    landed(name, l)
                    w = cols(in_slot[name])
                    for t in range(NT):
                        b = turn["pj"] % 4
                        turn["pj"] += 1
                        free(b, l)
                        for k in range(KD):
                            ins = mm(bank[b].t, hT[:, k, tok(t)], w[:, k, :], start=(k == 0), stop=(k == KD - 1))
                        filled(ins, b, (name, t))

                def attention(br, l):
                    if br == "f":
                        pe.wait_ge(cum_ready.sem, cum_ready.at("cum", l))
                        for t in range(NT):
                            for what in "qk":
                                in_sbuf(book.where[(br + what, t)], (br + what, t), l)
                    else:
                        pe.wait_ge(roped.sem, roped.at((br + "k", KB - 1), l))
                    if br == "s":
                        pe.wait_ge(keep_ready.sem, keep_ready.at("keep", l))
                    for t in range(NT):
                        in_sbuf(book.where[(br + "v", t)], (br + "v", t), l)

                    def scores(n):
                        p, t = divmod(n, NT)
                        W = width(t)
                        for j in range(2):
                            b = 2 * (n % 2) + j
                            rows = slice(HD * j, HD * j + HD)
                            free(b, l)
                            o = bank[b].t
                            part = br != "s" or t == 0
                            mm(o[:, 0:W], qT[rows, p, tok(t)], kT[rows, p, 0:W], start=True,
                               stop=part and br != "f")
                            if br == "f":
                                mm(o[:, 0:W], pick[:, 2 * p + j:2 * p + j + 1].to_broadcast([8, P]), cT[:, 0:W], start=False, stop=True)
                            if not part:
                                ins = mm(o[:, 0:W], identb, keep[:, (t - 1) * T:(t - 1) * T + W], start=False,
                                         stop=True)
                            else:
                                ins = mm(o[:, t * P:W], identb, causal_mask if br == "f" else chunk_mask,
                                         start=False, stop=True, skip_group_check=True)
                            filled(ins, b, ("score", br, n, j))

                    def turn_probs(n):
                        t = n % NT
                        pe.wait_ge(p_ready.sem, p_ready.at((br, n), l))
                        for j in range(1 if br == "d" else 2):
                            b = 4 + (n % 2 if br == "d" else j)
                            free(b, l)
                            for k in range(t + 1):
                                ins = nc.tensor.transpose(bank[b].t[:, k * P:(k + 1) * P],
                                                          pbuf[:, n % 2, j, k * P:(k + 1) * P], ident)
                            filled(ins, b, ("pt", br, n, j))

                    def values(n):
                        p, t = divmod(n, NT)
                        b = 6 + n % 2
                        free(b, l)
                        if br == "d":
                            in_sbuf(4 + n % 2, ("pt", br, n, 0), l)
                            for k in range(t + 1):
                                ins = mm(bank[b].t[:, 0:P], ptb[:, n % 2, k * P:(k + 1) * P], v[:, k, tok(p)],
                                         start=(k == 0), stop=(k == t))
                        else:
                            for j in range(2):
                                in_sbuf(4 + j, ("pt", br, n, j), l)
                                for k in range(t + 1):
                                    ins = mm(bank[b].t[j * HD:(j + 1) * HD, 0:P],
                                             v[:, k, (2 * p + j) * HD:(2 * p + j + 1) * HD],
                                             ptb[:, n % 2, j * 512 + k * P:j * 512 + (k + 1) * P],
                                             start=(k == 0), stop=(k == t))
                        filled(ins, b, ("o", br, n))

                    def turn_normed(n):
                        b = 6 + n % 2
                        free(b, l)
                        filled(nc.tensor.transpose(bank[b].t[:, 0:P], onorm[n % 2], ident), b, ("on", n))

                    for n in range(NSTEP + 4):
                        if n < NSTEP:
                            scores(n)
                        if 2 <= n < NSTEP + 2:
                            turn_probs(n - 2)
                        if 3 <= n < NSTEP + 3:
                            values(n - 3)
                        if br == "d" and n >= 4:
                            turn_normed(n - 4)

                def gated_output(br, l):
                    for n in (NSTEP - 2, NSTEP - 1):
                        b = 6 + n % 2
                        in_sbuf(b, ("on", n) if br == "d" else ("o", br, n), l)
                    landed(br + "g0", l)
                    landed(br + "br", l)
                    wb = cols(in_slot[br + "br"], KB)
                    for c in range(KD):
                        if c == 4:
                            landed(br + "g1", l)
                        w = cols(in_slot[br + "g0" if c < 4 else br + "g1"])
                        b = c % 2
                        free(b, l)
                        for k in range(KD):
                            ins = mm(bank[b].t, w[:, k, (c % 4) * P:(c % 4 + 1) * P], hT[:, k, :], start=(k == 0),
                                     stop=(k == KD - 1))
                        filled(ins, b, ("g", br, c))
                        free(2 + b, l)
                        for k in range(KB):
                            ins = mm(bank[2 + b].t, wb[:, k, c * P:(c + 1) * P], oT[:, k, :], start=(k == 0),
                                     stop=(k == KB - 1))
                        filled(ins, 2 + b, ("br", br, c))

                def output(l):
                    pe.wait_ge(y_ready.sem, y_ready.at("y", l))
                    landed("wo0", l)
                    landed("wo1", l)
                    for t in range(NT):
                        for half in range(2):
                            b = 4 + (2 * t + half) % 4
                            free(b, l)
                            for k in range(KD):
                                w = cols(in_slot["wo0" if k < KB else "wo1"], KB)
                                ins = mm(bank[b].t, yT[:, k, tok(t)], w[:, k % KB, half * 512:(half + 1) * 512],
                                         start=(k == 0), stop=(k == KD - 1))
                            filled(ins, b, ("m", t, half))
                        if t:
                            transpose_tile("ln1", t - 1, l)
                    transpose_tile("ln1", NT - 1, l)

                def transposed(key, l):
                    for t in (NT - 2, NT - 1):
                        for half in range(2):
                            in_sbuf(2 * (t % 2) + half, (key, t, half), l)

                def route(l):
                    transposed("ln1", l)
                    free(4, l)
                    for t in range(NT):
                        for k in range(KD):
                            ins = mm(bank[4].t[:, t * NEXP:(t + 1) * NEXP], hT[:, k, tok(t)], wr[:, k, :],
                                     start=(k == 0), stop=(k == KD - 1))
                    filled(ins, 4, "router")
                    pe.wait_ge(hot_ready.sem, hot_ready.at("hot", l))
                    free(5, l)
                    for t in range(NT + 1):
                        for u in range(min(t + 1, NT)):
                            ins = mm(bank[5].t[:, t * NEXP:(t + 1) * NEXP], tri if u == t else ones, both[:, u, :],
                                     start=(u == 0), stop=(u == min(t, NT - 1)))
                    filled(ins, 5, "rank")

                def turn_rows(n, b0, fill):
                    for half in range(2):
                        for k in range(4):
                            kd = 4 * half + k
                            ins = nc.tensor.transpose(bank[b0 + half].t[:, k * C:(k + 1) * C],
                                                      xin[n][:, kd * P:(kd + 1) * P], ident[0:C, 0:C])
                        fill(ins, half)

                def up(n, s, bnk, fill):
                    w = cols(s)
                    for f in range(FE):
                        for k in range(KD):
                            ins = mm(bank[bnk].t[:, f * C:(f + 1) * C], w[:, k, f * P:(f + 1) * P], xT[n][:, k, :],
                                     start=(k == 0), stop=(k == KD - 1))
                    fill(ins)

                def down(n, s, half, bnk):
                    w = cols(s, FE)
                    for f in range(FE):
                        ins = mm(bank[bnk].t[0:C, :], hid[n][:, f, :], w[:, f, half * 512:(half + 1) * 512],
                                 start=(f == 0), stop=(f == FE - 1))
                    return ins

                def expert_rows(n, landed_at, l, i=0):
                    pe.wait_ge(xin_land[n].sem, landed_at)
                    free(0, l, i)
                    free(1, l, i)
                    turn_rows(n, 0, lambda ins, half: filled(ins, half, (book.scope, "x", n, half)))

                def expert_pair(l, i):
                    def rows(n):
                        landed_at = xin_land[n].start(l, i)
                        expert_rows(n, landed_at if n else landed_at + 16, l, i)

                    def gate_up(n):
                        free(0, l, i)
                        free(1, l, i)
                        for m in range(2):
                            s, b = 3 * n + m, 2 + 2 * n + m
                            pe.wait_ge(land[s].sem, land[s].at(("first", s), l) + i * land[s].total["pair"])
                            free(b, l, i)
                            up(n, s, b, lambda ins: filled(ins, b, ("gu", n, m)))

                    def down_(n):
                        s = 3 * n + 2
                        pe.wait_ge(land[s].sem, land[s].at(("first", s), l) + i * land[s].total["pair"])
                        in_sbuf(3 + 2 * n, ("gu", n, 1), l, i)
                        for half in range(2):
                            free(6 + half, l, i)
                            filled(down(n, s, half, 6 + half), 6 + half, ("y", n, half))

                    gate_up(0)
                    rows(1)
                    down_(0)
                    gate_up(1)
                    rows(0)
                    down_(1)

                def over_block(l, j, b):
                    pe.wait_ge(over_x.sem, over_x.value("over", 16, 0, b))
                    for half in range(2):
                        for k in range(4):
                            kd = 4 * half + k
                            ins = nc.tensor.transpose(bank[half].t[:, k * C:(k + 1) * C],
                                                      xin[0][:, kd * P:(kd + 1) * P], ident[0:C, 0:C])
                    ins.then_inc(over_t.sem, over_t.tick())
                    pe.wait_ge(over_w.sem, over_w.value("over", 48, 0, b))
                    pe.wait_ge(over_xT.sem, over_xT.value("over", 1, 0, b))
                    up(0, 0, 2, lambda ins: None)
                    up(0, 1, 3, lambda ins: ins.then_inc(over_gu.sem, over_gu.tick()))
                    pe.wait_ge(over_h.sem, over_h.value("over", 1, 0, b))
                    down(0, 2, 0, 6)
                    down(0, 2, 1, 7).then_inc(over_y.sem, over_y.tick())
                    pe.wait_ge(over_ye.sem, over_ye.value("over", 1, 0, b))

                book.scope = "pre"
                pe.wait_ge(const_land.sem, const_land.at("all"))
                transpose_h("ln0")
                for b in range(4, 8):
                    pe.sem_inc(bank[b].full.sem, bank[b].full.tick())
                    pe.sem_inc(bank[b].read, 1)
                pe.sem_inc(over_y.sem, over_y.tick())
                count_blocks(pe)
                with pe.Fori(0, DEPTH) as l:
                    book.scope = "layer"
                    for b in range(4):
                        pe.wait_ge(bank[b].read, bank[b].full.now(l))
                    index_logits(l)
                    forget_logits(l)
                    for br_ in BRANCHES:
                        queries_keys_values(br_, l)
                        attention(br_, l)
                        gated_output(br_, l)
                        turn["pj"] = 0
                    output(l)
                    route(l)
                    expert_rows(0, xin_land[0].start(l) + 16, l)
                    with pe.Fori(0, NPAIR) as i:
                        book.scope = "pair"
                        expert_pair(l, i)
                    book.scope = "tail"
                    for b in range(8):
                        pe.wait_ge(bank[b].read, bank[b].full.now(l))
                    overflow(pe, l, lambda j, b: over_block(l, j, b))
                    transpose_h("ln2", l)

            @block.scalar
            def _(act):
                rope_n = [0]

                def filled(b, key, l=0, i=NPAIR - 1):
                    act.wait_ge(bank[b].full.sem, bank[b].full.at(key, l, i))

                def in_sbuf(b, key, l=0, i=NPAIR - 1):
                    act.wait_ge(bank[b].read, bank[b].full.at(key, l, i))

                def copy(dst, b, src, scale=1.0):
                    nc.scalar.activation(dst, src, ACT.Copy, scale=scale).then_inc(bank[b].read, 1)

                def take_hT(key, l=0):
                    for t in range(NT):
                        for half in range(2):
                            b = 2 * (t % 2) + half
                            filled(b, (key, t, half), l)
                            copy(hT[:, 4 * half:4 * half + 4, tok(t)], b,
                                 bank[b].t.rearrange("p (k c) -> p k c", c=P))

                def take_z(key, l, scale=1.0, after=None):
                    r = rope_n[0]
                    rope_n[0] += 1
                    b = book.where.get(key, 0)
                    filled(b, key, l)
                    if r >= 2:
                        act.wait_ge(roped.sem, roped.at(("n", r - 2), l))
                    copy(z[r % 2], b, bank[b].t, scale)

                def take_projections(br, l):
                    if br != "f":
                        for c in (KD - 2, KD - 1):
                            before = BRANCHES[BRANCHES.index(br) - 1]
                            in_sbuf(2 + c % 2, ("br", before, c), l)
                    for what in "qk":
                        for n in range(KB):
                            key = (br + what, n)
                            sc = SCALE if what == "q" else 1.0
                            if br == "f":
                                b = book.where.get(key, 0)
                                filled(b, key, l)
                                copy((qT if what == "q" else kT)[:, n, :], b, bank[b].t, sc)
                            else:
                                take_z(key, l, sc)
                    for t in range(NT):
                        b = book.where.get((br + "v", t), 0)
                        filled(b, (br + "v", t), l)
                        copy(v[:, t, :], b, bank[b].t)

                def attention(br, l):
                    for n in range(NSTEP + 4):
                        if n < NSTEP:
                            W = width(n % NT)
                            act.wait_ge(max_ready.sem, max_ready.at((br, n), l))
                            if n >= 2:
                                for j in range(1 if br == "d" else 2):
                                    filled(4 + (n % 2 if br == "d" else j), ("pt", br, n - 2, j), l)
                            for j in range(2):
                                b = 2 * (n % 2) + j
                                nc.scalar.activation(pbuf[:, n % 2, j, 0:W], bank[b].t[:, 0:W], ACT.Exp,
                                                     bias=neg_max[n % 2][:, j:j + 1],
                                                     accum_out=psum_row[n % 2][:, j:j + 1]).then_inc(bank[b].read, 1)
                        if 2 <= n < NSTEP + 2:
                            m = n - 2
                            b = 4 + (m % 2 if br == "d" else 0)
                            filled(b, ("pt", br, m, 0), l)
                            if m >= 2:
                                filled(6 + m % 2, ("o", br, m - 2), l)
                            copy(ptb[:, m % 2, 0:width(m % NT)], b, bank[b].t[:, 0:width(m % NT)])
                        if 3 <= n < NSTEP + 3:
                            m = n - 3
                            b = 6 + m % 2
                            filled(b, ("o", br, m), l)
                            if br == "d":
                                nc.scalar.activation(bank[b].t[:, P:2 * P], bank[b].t[:, 0:P], ACT.Square,
                                                     accum_out=ssq[m % 2]).then_inc(ssq_ready.sem, ssq_ready.tick(m))
                            else:
                                copy(oT[:, m // NT, tok(m % NT)], b, bank[b].t[:, 0:P])
                        if br == "d" and n >= 4:
                            m = n - 4
                            b = 6 + m % 2
                            filled(b, ("on", m), l)
                            copy(oT[:, m // NT, tok(m % NT)], b, bank[b].t[:, 0:P])

                def gates(br, l):
                    for c in range(KD):
                        b = c % 2
                        filled(b, ("g", br, c), l)
                        if c >= 2:
                            in_sbuf(2 + b, ("br", br, c - 2), l)
                        nc.scalar.activation(gate[b], bank[b].t, ACT.Sigmoid).then_inc(bank[b].read, 1)

                book.scope = "pre"
                take_hT("ln0")
                act.wait_ge(angle_ready.sem, angle_ready.at("angles"))
                nc.scalar.activation(sin, z[0], ACT.Sin).then_inc(act_seq.sem, act_seq.tick())
                nc.scalar.activation(cos, z[1], ACT.Sin).then_inc(act_seq.sem, act_seq.tick("trig"))
                count_blocks(act)
                with act.Fori(0, DEPTH) as l:
                    book.scope = "layer"
                    rope_n[0] = 0
                    act.wait_ge(h_ready.sem, h_ready.start(l))
                    act.wait_ge(dve_seq.sem, dve_seq.at("trig"))
                    for key in ("iq0", "iq1", "ik"):
                        take_z(key, l)
                    m = 0
                    for t in range(1, NT):
                        for hd in range(IDX_H):
                            filled(hd, ("logit", t, hd), l)
                            if m >= 2:
                                act.wait_ge(dve_seq.sem, dve_seq.at(("weighed", m - 2), l))
                            nc.scalar.activation(relu[m % 2][:, 0:width(t)], bank[hd].t[:, 0:width(t)],
                                                 ACT.Relu).then_inc(bank[hd].read, 1)
                            m += 1
                    act.wait_ge(lam_prod.sem, lam_prod.at("lam", l))
                    nc.scalar.activation(lamw[:, 4:6], lamw[:, 2:4], ACT.Exp).then_inc(lam_exp.sem, lam_exp.tick("lam"))
                    act.wait_ge(ffe_ready.sem, ffe_ready.at("ffe", l))
                    nc.scalar.activation(ffe, ffe, ACT.Exp).then_inc(act_seq.sem, act_seq.tick())
                    act.wait_ge(act_seq.sem, act_seq.now(l))
                    nc.scalar.activation(ffe, ffe, ACT.Ln, bias=1.0).then_inc(ffl_ready.sem, ffl_ready.tick("ffl"))
                    for br_ in BRANCHES:
                        take_projections(br_, l)
                        attention(br_, l)
                        gates(br_, l)
                    take_hT("ln1", l)
                    filled(4, "router", l)
                    nc.scalar.activation(aff, bank[4].t[:, 0:P].rearrange("p (t e) -> p t e", e=NEXP),
                                         ACT.Sigmoid).then_inc(bank[4].read, 1)

                    def rows(n, i=0):
                        filled(0, (book.scope, "x", n, 0), l, i)
                        copy(xT[n][:, 0:4, :], 0, bank[0].t[:, 0:4 * C].rearrange("p (k c) -> p k c", c=C))

                    rows(0)
                    with act.Fori(0, NPAIR) as i:
                        book.scope = "pair"


                        def silu(n):
                            b = 2 + 2 * n
                            filled(b, ("gu", n, 0), l, i)
                            nc.scalar.activation(act_g[n], bank[b].t[:, 0:FE * C].rearrange("p (k c) -> p k c", c=C),
                                                 ACT.Silu).then_inc(bank[b].read, 1)

                        def y_half(n):
                            filled(6, ("y", n, 0), l, i)
                            act.wait_ge(ysb_free[n].sem, ysb_free[n].start(l, i))
                            copy(ysb[n][:, 0:512], 6, bank[6].t[0:C, :])

                        silu(0)
                        rows(1, i)
                        y_half(0)
                        silu(1)
                        rows(0, i)
                        y_half(1)
                    book.scope = "tail"

                    def over_silu(j, b):
                        act.wait_ge(over_gu.sem, over_gu.value("over", 1, 0, b))
                        nc.scalar.activation(act_g[0], bank[2].t[:, 0:FE * C].rearrange("p (k c) -> p k c", c=C),
                                             ACT.Silu).then_inc(over_act.sem, over_act.tick())

                    overflow(act, l, over_silu)
                    take_hT("ln2", l)

            @block.vector
            def _(dve):
                V = nc.vector

                def link(ins, l=0, i=NPAIR - 1, key=None):
                    ins.then_inc(dve_seq.sem, dve_seq.tick(key))
                    dve.wait_ge(dve_seq.sem, dve_seq.now(l, i))

                def filled(b, key, l=0, i=NPAIR - 1):
                    dve.wait_ge(bank[b].full.sem, bank[b].full.at(key, l, i))

                def in_sbuf(b, key, l=0, i=NPAIR - 1):
                    dve.wait_ge(bank[b].read, bank[b].full.at(key, l, i))

                def layer_norm(key, l, source):
                    for t in range(NT + 1):
                        if t < NT:
                            source(t)
                            for half in range(2):
                                ins = V.bn_stats(stats[:, t, half, :], h[:, t, half * 512:(half + 1) * 512])
                                ins.then_inc(dve_seq.sem, dve_seq.tick())
                            dve.wait_ge(dve_seq.sem, dve_seq.now(l))
                            alone(dve)
                            V.bn_aggr(moments[:, t, :], stats[:, t, :, :]).then_inc(
                                moments_ready.sem, moments_ready.tick((key, t)))
                        if t == 1 and key != "ln0":
                            dve.wait_ge(ln_land.sem, ln_land.at(key, l))
                        if t:
                            u = t - 1
                            dve.wait_ge(rstd_ready.sem, rstd_ready.at((key, u), l))
                            link(V.scalar_tensor_tensor(h[:, u, :], h[:, u, :], moments[:, u, 0:1], ln_g,
                                                        ALU.subtract, ALU.mult), l)
                            V.scalar_tensor_tensor(h[:, u, :], h[:, u, :], rstd[:, u:u + 1], ln_b,
                                                   ALU.mult, ALU.add).then_inc(h_ready.sem, h_ready.tick((key, u)))

                def rope(r, key, src_key, dst, l):
                    zb = book.where.get(src_key, 0)
                    in_sbuf(zb, src_key, l)
                    V.tensor_tensor(r1, z[r % 2], cos, ALU.mult).then_inc(dve_seq.sem, dve_seq.tick())
                    b = 4 + r % 2
                    filled(b, ("rope", r), l)
                    V.tensor_tensor(r2, bank[b].t, sin, ALU.mult).then_inc(bank[b].read, 1)
                    dve.wait_ge(dve_seq.sem, dve_seq.now(l))
                    in_sbuf(b, ("rope", r), l)
                    V.tensor_tensor(dst, r1, r2, ALU.add).then_inc(roped.sem, roped.tick(("n", r)))
                    roped.marks[key] = roped.marks[("n", r)]
                    dve.wait_ge(roped.sem, roped.now(l))

                def index_scores(l):
                    m = 0
                    for t in range(1, NT):
                        W = width(t)
                        for hd in range(IDX_H):
                            in_sbuf(hd, ("logit", t, hd), l)
                            w1 = iw[:, t, hd:hd + 1]
                            if hd == 0:
                                ins = V.tensor_scalar(score[t], relu[m % 2][:, 0:W], w1, None, ALU.mult)
                            else:
                                ins = V.scalar_tensor_tensor(score[t], relu[m % 2][:, 0:W], w1, score[t], ALU.mult,
                                                             ALU.add)
                            link(ins, l, key=("weighed", m))
                            m += 1
                        link(V.tensor_tensor(score[t][:, t * P:W], score[t][:, t * P:W], chunk_mask, ALU.add), l)

                def forget_sums(l):
                    b = book.where.get("ff", 0)
                    filled(b, "ff", l)
                    dve.wait_ge(small_land.sem, small_land.at("all", l))
                    V.tensor_scalar(ffx, bank[b].t[0:8, :], b_f[:, 0:1], None, ALU.add).then_inc(bank[b].read, 1)
                    in_sbuf(b, "ff", l)
                    V.scalar_tensor_tensor(ffe, ffx, -1.0, ffx, ALU.mult, ALU.min).then_inc(
                        ffe_ready.sem, ffe_ready.tick("ffe"))
                    dve.wait_ge(ffl_ready.sem, ffl_ready.at("ffl", l))
                    link(V.scalar_tensor_tensor(ffx, ffx, 0.0, ffe, ALU.min, ALU.subtract), l)
                    V.tensor_tensor_scan(cT[:, :], zeros[0:8, 0:1].to_broadcast([8, T]), ffx, 0.0, ALU.add, ALU.add).then_inc(
                        cum_ready.sem, cum_ready.tick("cum"))

                def pick_keys(l):
                    for t in range(1, NT):
                        for _ in range(TOPK // 8):
                            alone(dve)
                            link(V.max(top8, score[t]), l)
                            alone(dve)
                            link(V.match_replace(score[t], top8, score[t], TAKEN), l)
                        V.tensor_scalar(keep[:, (t - 1) * T:(t - 1) * T + width(t)], score[t], 0.5 * TAKEN, NEG,
                                        ALU.is_gt, ALU.mult).then_inc(keep_ready.sem, keep_ready.tick("keep"))

                def lambdas(l):
                    dve.wait_ge(lam_exp.sem, lam_exp.at("lam", l))
                    link(V.tensor_tensor(lamw[:, 6:7], lamw[:, 5:6], lamw[:, 4:5], ALU.subtract), l)
                    V.tensor_tensor(neg_lam, lamw[:, 6:7], laminit[:, 0:1], ALU.subtract).then_inc(
                        dve_seq.sem, dve_seq.tick())
                    link(V.tensor_scalar(norm_g[:, :], norm_g[:, :], laminit[:, 1:2], None, ALU.mult), l)

                def attention(br, l):
                    def row_max(n):
                        W = width(n % NT)
                        b = 2 * (n % 2)
                        filled(b, ("score", br, n, 0), l)
                        filled(b + 1, ("score", br, n, 1), l)
                        V.tensor_reduce(neg_max[n % 2], ps[:, b:b + 2, 0:W], AX.X, ALU.max, negate=True).then_inc(
                            max_ready.sem, max_ready.tick((br, n)))

                    def normalise(n):
                        W = width(n % NT)
                        b = 2 * (n % 2)
                        r = rcp[n % 2]
                        pb = [pbuf[:, n % 2, j, 0:W] for j in range(2)]
                        in_sbuf(b, ("score", br, n, 0), l)
                        in_sbuf(b + 1, ("score", br, n, 1), l)
                        link(V.reciprocal(r, psum_row[n % 2]), l)
                        if br == "d":
                            link(V.tensor_tensor(rcl[n % 2], r[:, 1:2], neg_lam, ALU.mult), l)
                            link(V.tensor_scalar(pb[1], pb[1], rcl[n % 2], None, ALU.mult), l)
                            V.scalar_tensor_tensor(pb[0], pb[0], r[:, 0:1], pb[1], ALU.mult, ALU.add).then_inc(
                                p_ready.sem, p_ready.tick((br, n)))
                        else:
                            for j in range(2):
                                V.tensor_scalar(pb[j], pb[j], r[:, j:j + 1], None, ALU.mult).then_inc(
                                    p_ready.sem, p_ready.tick((br, n)))

                    def take_probs(n):
                        W = width(n % NT)
                        filled(5, ("pt", br, n, 1), l)
                        if n >= 2:
                            filled(6 + n % 2, ("o", br, n - 2), l)
                        V.tensor_copy(ptb[:, n % 2, 512:512 + W], bank[5].t[:, 0:W]).then_inc(bank[5].read, 1)

                    def head_norm(n):
                        b = 6 + n % 2
                        dve.wait_ge(rms_ready.sem, rms_ready.at(n, l))
                        filled(b, ("o", br, n), l)
                        V.scalar_tensor_tensor(onorm[n % 2], bank[b].t[:, 0:P], rms[n % 2], norm_g[:, :], ALU.mult,
                                               ALU.mult).then_inc(bank[b].read, 1)

                    for n in range(NSTEP + 3):
                        if n < NSTEP:
                            row_max(n)
                        if 1 <= n < NSTEP + 1:
                            normalise(n - 1)
                        if br != "d" and 2 <= n < NSTEP + 2:
                            take_probs(n - 2)
                        if br == "d" and n >= 3:
                            head_norm(n - 3)

                def gated_sum(br, l):
                    if br == BRANCHES[0]:
                        dve.wait_ge(zero_land.sem, zero_land.at("all"))
                    for c in range(KD):
                        b = c % 2
                        in_sbuf(b, ("g", br, c), l)
                        filled(2 + b, ("br", br, c), l)
                        dst = yT[:, c, :] if br == BRANCHES[0] else prod
                        V.tensor_tensor(dst, gate[b], bank[2 + b].t, ALU.mult).then_inc(bank[2 + b].read, 1)
                        in_sbuf(2 + b, ("br", br, c), l)
                        if br != BRANCHES[0]:
                            V.tensor_tensor(yT[:, c, :], yT[:, c, :], prod, ALU.add).then_inc(
                                y_ready.sem, y_ready.tick("y"))
                            dve.wait_ge(y_ready.sem, y_ready.now(l))

                def mixer_rows(l):
                    def source(t):
                        for half in range(2):
                            b = 4 + (2 * t + half) % 4
                            filled(b, ("m", t, half), l)
                            hh = h[:, t, half * 512:(half + 1) * 512]
                            V.scalar_tensor_tensor(hh, hh, ALPHA, bank[b].t, ALU.mult, ALU.add).then_inc(
                                bank[b].read, 1)
                            in_sbuf(b, ("m", t, half), l)
                    return source

                def route(l):
                    L = lambda ins: link(ins, l)

                    def N(ins):
                        ins.then_inc(dve_seq.sem, dve_seq.tick())

                    in_sbuf(4, "router", l)
                    N(V.memset(gsc[:, :, :], NEG))
                    for t in range(NT):
                        N(V.tensor_tensor(sel[:, t, :], aff[:, t, :], br[:, :], ALU.add))
                    dve.wait_ge(dve_seq.sem, dve_seq.now(l))
                    alone(dve)
                    for g in range(NT * NGRP):
                        N(V.max(srt[:, g, :], sel.rearrange("p t e -> p (t e)")[:, g * EPG:(g + 1) * EPG]))
                    dve.wait_ge(dve_seq.sem, dve_seq.now(l))
                    L(V.tensor_tensor(gsc[:, :, 0:NGRP], srt[:, :, 0].rearrange("p (t g) -> p t g", g=NGRP),
                                      srt[:, :, 1].rearrange("p (t g) -> p t g", g=NGRP), ALU.add))
                    alone(dve)
                    for t in range(NT):
                        N(V.max(gtop[:, t, :], gsc[:, t, :]))
                    dve.wait_ge(dve_seq.sem, dve_seq.now(l))
                    alone(dve)
                    for t in range(NT):
                        N(V.max_index(gidx[:, t, :], gtop[:, t, :], gsc[:, t, :]))
                    dve.wait_ge(dve_seq.sem, dve_seq.now(l))
                    L(V.tensor_copy(gidf, gidx[:, :, 0]))
                    for t in range(NT):
                        N(V.tensor_scalar(gm[:, t, :], iota_g, gidf[:, t:t + 1], None, ALU.is_equal))
                    dve.wait_ge(dve_seq.sem, dve_seq.now(l))
                    N(V.tensor_scalar(tmp, gm, -NEG, NEG, ALU.mult, ALU.add))
                    L(V.tensor_tensor(sel, sel, gm, ALU.mult))
                    L(V.tensor_tensor(sel, sel, tmp, ALU.add))
                    alone(dve)
                    for t in range(NT):
                        N(V.max(etop[:, t, :], sel[:, t, :]))
                    dve.wait_ge(dve_seq.sem, dve_seq.now(l))
                    alone(dve)
                    for t in range(NT):
                        N(V.max_index(eidx[:, t, :], etop[:, t, :], sel[:, t, :]))
                    dve.wait_ge(dve_seq.sem, dve_seq.now(l))
                    for k in range(2):
                        N(V.tensor_copy(eidf[:, k, :], eidx[:, :, k]))
                    dve.wait_ge(dve_seq.sem, dve_seq.now(l))
                    for k in range(2):
                        for t in range(NT):
                            N(V.tensor_scalar(hot[:, k, t, :], iota_e, eidf[:, k, t:t + 1], None, ALU.is_equal))
                    dve.wait_ge(dve_seq.sem, dve_seq.now(l))
                    V.tensor_tensor(both, hot[:, 0], hot[:, 1], ALU.add).then_inc(hot_ready.sem, hot_ready.tick("hot"))
                    for k in range(2):
                        N(V.tensor_tensor((tmp, gm)[k], hot[:, k], aff, ALU.mult))
                    dve.wait_ge(dve_seq.sem, dve_seq.now(l))
                    for k in range(2):
                        N(V.tensor_reduce(wts[:, k, :], (tmp, gm)[k], AX.X, ALU.add))
                    dve.wait_ge(dve_seq.sem, dve_seq.now(l))
                    L(V.tensor_tensor(wsum[:, 0, :], wts[:, 0, :], wts[:, 1, :], ALU.add))
                    L(V.reciprocal(wsum[:, 1, :], wsum[:, 0, :]))
                    for k in range(2):
                        N(V.tensor_tensor(wts_keep[:, k, :], wts[:, k, :], wsum[:, 1, :], ALU.mult))
                    filled(5, "rank", l)
                    for k in range(2):
                        N(V.tensor_tensor((tmp, gm)[k], hot[:, k],
                                          bank[5].t[:, 0:P].rearrange("p (t e) -> p t e", e=NEXP), ALU.mult))
                    V.tensor_copy(cum, bank[5].t[:, P:P + NEXP]).then_inc(bank[5].read, 1)
                    dve.wait_ge(dve_seq.sem, dve_seq.now(l))
                    for k in range(2):
                        N(V.tensor_reduce(rank[:, k, :], (tmp, gm)[k], AX.X, ALU.add))
                    in_sbuf(5, "rank", l)
                    L(V.tensor_scalar(ovc, cum, float(C), None, ALU.is_gt))
                    L(V.tensor_scalar(quo, rank, float(C), None, ALU.is_ge))
                    N(V.tensor_copy(r8b, quo))
                    for q in range(2, OVQ + 1):
                        N(V.scalar_tensor_tensor(ovc, cum, float(q * C), ovc, ALU.is_gt, ALU.add))
                        L(V.scalar_tensor_tensor(quo, rank, float(q * C), quo, ALU.is_ge, ALU.add))
                    L(V.tensor_tensor_scan(cum, zeros[:, 0:NEXP], ovc, 0.0, ALU.add, ALU.add))
                    L(V.tensor_tensor(base, cum, ovc, ALU.subtract))
                    for k in range(2):
                        for t in range(NT):
                            N(V.tensor_tensor((tmp, gm)[k][:, t, :], hot[:, k, t, :], base, ALU.mult))
                    dve.wait_ge(dve_seq.sem, dve_seq.now(l))
                    for k in range(2):
                        N(V.tensor_reduce(bas[:, k, :], (tmp, gm)[k], AX.X, ALU.add))
                    dve.wait_ge(dve_seq.sem, dve_seq.now(l))
                    L(V.scalar_tensor_tensor(r8a, bas, float(NEXP - 1), quo, ALU.add, ALU.add))
                    L(V.tensor_tensor(r8a, r8a, eidf, ALU.subtract))
                    L(V.tensor_tensor(r8a, r8a, r8b, ALU.mult))
                    L(V.tensor_tensor(r8a, r8a, eidf, ALU.add))
                    L(V.scalar_tensor_tensor(slotf, quo, -float(C), rank, ALU.mult, ALU.add))
                    L(V.scalar_tensor_tensor(slotf, r8a, float(C), slotf, ALU.mult, ALU.add))
                    V.tensor_copy(slot_keep[:, :, :], slotf).then_inc(slot_ready.sem, slot_ready.tick("slot"))
                    for j in range(NOV):
                        N(V.tensor_scalar(ovt[:, j, :], cum[0:1, :], float(j), None, ALU.is_le))
                    dve.wait_ge(dve_seq.sem, dve_seq.now(l))
                    L(V.tensor_reduce(schedf[:, 1:1 + NOV], ovt, AX.X, ALU.add))
                    L(V.tensor_scalar(schedf[:, 1:1 + NOV], schedf[:, 1:1 + NOV], float(NEXP - 1), None, ALU.min))
                    L(V.tensor_copy(schedf[:, 0:1], cum[0:1, NEXP - 1:NEXP]))
                    V.tensor_copy(sched[:, :], schedf).then_inc(sched_ready.sem, sched_ready.tick("sched"))

                def combine(l):
                    def source(t):
                        n = t % 2
                        dve.wait_ge(got_land[n].sem, got_land[n].at(t, l))
                        link(V.tensor_scalar(got[n][1], got[n][1], wts_keep[:, 1, t:t + 1], None, ALU.mult), l)
                        link(V.scalar_tensor_tensor(got[n][0], got[n][0], wts_keep[:, 0, t:t + 1], got[n][1],
                                                    ALU.mult, ALU.add), l)
                        V.scalar_tensor_tensor(h[:, t, :], h[:, t, :], ALPHA, got[n][0], ALU.mult, ALU.add).then_inc(
                            got_used.sem, got_used.tick(t))
                        dve.wait_ge(got_used.sem, got_used.now(l))
                    return source

                book.scope = "pre"
                dve.wait_ge(const_land.sem, const_land.at("all"))
                dve.wait_ge(x_land.sem, x_land.at("all"))
                layer_norm("ln0", 0, lambda t: None)
                dve.wait_ge(pos_land.sem, pos_land.at("all"))
                link(V.tensor_copy(z[0], r1.bitcast(I32)))
                link(V.tensor_scalar(z[0], z[0], inv_freq, None, ALU.mult))
                link(V.tensor_scalar(r2, z[0], 1 / (2 * math.pi), MAGIC, ALU.mult, ALU.add))
                link(V.tensor_scalar(r2, r2, MAGIC, None, ALU.subtract))
                for c in (C1, C2, C3):
                    link(V.scalar_tensor_tensor(z[0], r2, -c, z[0], ALU.mult, ALU.add))
                link(V.tensor_scalar(z[1], z[0], math.pi / 2, None, ALU.add))
                link(V.tensor_scalar(r2, z[1], math.pi, -2 * math.pi, ALU.is_gt, ALU.mult))
                link(V.tensor_tensor(z[1], z[1], r2, ALU.add))
                link(V.tensor_scalar(z[1], z[1], -PI_LO, PI_LO, ALU.max, ALU.min))
                V.tensor_scalar(z[0], z[0], -PI_LO, PI_LO, ALU.max, ALU.min).then_inc(
                    angle_ready.sem, angle_ready.tick("angles"))
                dve.wait_ge(act_seq.sem, act_seq.at("trig"))
                link(V.tensor_scalar(sin, sin, sign_half, None, ALU.mult), key="trig")
                dve.wait_ge(pool_seq.sem, pool_seq.at("zeros"))
                count_blocks(dve)
                with dve.Fori(0, DEPTH) as l:
                    book.scope = "layer"
                    b_iw = book.where.get("iw", 0)
                    filled(b_iw, "iw", l)
                    V.tensor_scalar(iw[:, :, :], bank[b_iw].t[:, 0:NT * IDX_H].rearrange("p (t c) -> p t c", c=IDX_H),
                                    (IDX_H * HD) ** -0.5, None, ALU.mult).then_inc(bank[b_iw].read, 1)
                    in_sbuf(b_iw, "iw", l)
                    for r, (key, dst) in enumerate((("iq0", iqT[:, 0, :]), ("iq1", iqT[:, 1, :]), ("ik", ikT))):
                        rope(r, key, key, dst, l)
                    index_scores(l)
                    dve.wait_ge(small_land.sem, small_land.at("all", l))
                    pairs = lamv[:, :, :].rearrange("p (a b) d -> p a b d", b=2)
                    link(V.tensor_tensor(pairs[:, :, 0, :], pairs[:, :, 0, :], pairs[:, :, 1, :], ALU.mult), l)
                    V.tensor_reduce(lamw[:, 2:4], pairs[:, :, 0, :], AX.X, ALU.add).then_inc(
                        lam_prod.sem, lam_prod.tick("lam"))
                    forget_sums(l)
                    lambdas(l)
                    pick_keys(l)
                    r = 3
                    for br_ in BRANCHES:
                        if br_ != "f":
                            for what, dst in (("q", qT), ("k", kT)):
                                for n in range(KB):
                                    rope(r, (br_ + what, n), (br_ + what, n), dst[:, n, :], l)
                                    r += 1
                        attention(br_, l)
                        gated_sum(br_, l)
                    layer_norm("ln1", l, mixer_rows(l))
                    route(l)

                    def rows(n, i=0):
                        filled(1, (book.scope, "x", n, 1), l, i)
                        V.tensor_copy(xT[n][:, 4:8, :], bank[1].t[:, 0:4 * C].rearrange(
                            "p (k c) -> p k c", c=C)).then_inc(bank[1].read, 1)

                    rows(0)
                    with dve.Fori(0, NPAIR) as i:
                        book.scope = "pair"

                        def hidden(n):
                            b = 3 + 2 * n
                            in_sbuf(b - 1, ("gu", n, 0), l, i)
                            filled(b, ("gu", n, 1), l, i)
                            V.tensor_tensor(hid[n], act_g[n], bank[b].t[:, 0:FE * C].rearrange(
                                "p (k c) -> p k c", c=C), ALU.mult).then_inc(bank[b].read, 1)

                        def y_half(n):
                            filled(7, ("y", n, 1), l, i)
                            dve.wait_ge(ysb_free[n].sem, ysb_free[n].start(l, i))
                            V.tensor_copy(ysb[n][:, 512:1024], bank[7].t[0:C, :]).then_inc(bank[7].read, 1)

                        hidden(0)
                        rows(1, i)
                        y_half(0)
                        hidden(1)
                        rows(0, i)
                        y_half(1)
                    book.scope = "tail"
                    for n in range(2):
                        dve.wait_ge(y_stored[n].sem, y_stored[n].at("y", l))

                    def over_block(j, b):
                        dve.wait_ge(over_t.sem, over_t.value("over", 1, 0, b))
                        for half in range(2):
                            ins = V.tensor_copy(xT[0][:, 4 * half:4 * half + 4, :],
                                                bank[half].t[:, 0:4 * C].rearrange("p (k c) -> p k c", c=C))
                        ins.then_inc(over_xT.sem, over_xT.tick())
                        dve.wait_ge(over_act.sem, over_act.value("over", 1, 0, b))
                        V.tensor_tensor(hid[0], act_g[0], bank[3].t[:, 0:FE * C].rearrange("p (k c) -> p k c", c=C),
                                        ALU.mult).then_inc(over_h.sem, over_h.tick())
                        dve.wait_ge(over_y.sem, over_y.value("over", 1, 0, b))
                        V.tensor_copy(ysb[0][:, 0:512], bank[6].t[0:C, :])
                        V.tensor_copy(ysb[0][:, 512:1024], bank[7].t[0:C, :]).then_inc(over_ye.sem, over_ye.tick())

                    overflow(dve, l, over_block)
                    layer_norm("ln2", l, combine(l))

            @block.gpsimd
            def _(pool):
                G = nc.gpsimd

                def inverse_roots(key, l=0):
                    for t in range(NT):
                        pool.wait_ge(moments_ready.sem, moments_ready.at((key, t), l))
                        alone(pool)
                        G.tensor_scalar(lameps[:, t:t + 1], moments[:, t, 1:2], EPS, None, ALU.add).then_inc(
                            pool_seq.sem, pool_seq.tick())
                        pool.wait_ge(pool_seq.sem, pool_seq.now(l))
                        alone(pool)
                        G.tensor_tensor(rstd[:, t:t + 1], lameps[:, t:t + 1], m_half, ALU.pow).then_inc(
                            rstd_ready.sem, rstd_ready.tick((key, t)))

                def norm_params(key, g, b, l):
                    for src, dst in ((g, ln_g), (b, ln_b)):
                        pool.dma_start(dst, src[bass.ds(l, 1), :].rearrange("o c -> (o c)").partition_broadcast(P)
                                       ).then_inc(ln_land.sem, ln_land.tick(key, 16))

                def load_rows(l, n, blk, i=NPAIR - 1):
                    pool.dma_start(xin[n], x_rows[blk, :]).then_inc(xin_land[n].sem, xin_land[n].tick("x", 16))

                book.scope = "pre"
                for sig in ysb_free:
                    pool.sem_inc(sig.sem, sig.tick())
                G.memset(zeros[:, :], 0.0).then_inc(pool_seq.sem, pool_seq.tick("zeros"))
                pool.wait_ge(pool_seq.sem, pool_seq.now())
                alone(pool)
                pool.wait_ge(const_land.sem, const_land.at("all"))
                alone(pool)
                inverse_roots("ln0")
                pool.wait_ge(land[RING - 1].sem, land[RING - 1].at(pieces[RING - 1]))
                alone(pool)
                G.memset(zero_row, 0.0).then_inc(pool_seq.sem, pool_seq.tick())
                pool.wait_ge(pool_seq.sem, pool_seq.now())
                for dst in (x_rows, y_rows[NEXP * C:, :]):
                    n, rest = divmod(dst.shape[0], P)
                    pool.dma_start(dst[0:n * P, :].rearrange("(n p) d -> p n d", p=P),
                                   zero_row.unsqueeze(1).to_broadcast([P, n, D])).then_inc(
                        zero_land.sem, zero_land.tick("all", 16))
                    if rest:
                        pool.dma_start(dst[n * P:, :], zero_row[0:rest, :]).then_inc(
                            zero_land.sem, zero_land.tick("all", 16))
                count_blocks(pool)
                with pool.Fori(0, DEPTH) as l:
                    book.scope = "layer"
                    for n in range(NSTEP):
                        pool.wait_ge(ssq_ready.sem, ssq_ready.at(n, l))
                        alone(pool)
                        G.tensor_scalar(rms_t[n % 2], ssq[n % 2], 1.0 / P, EPS, ALU.mult, ALU.add).then_inc(
                            pool_seq.sem, pool_seq.tick())
                        pool.wait_ge(pool_seq.sem, pool_seq.now(l))
                        alone(pool)
                        G.tensor_tensor(rms[n % 2], rms_t[n % 2], m_half, ALU.pow).then_inc(
                            rms_ready.sem, rms_ready.tick(n))
                    for n in (NSTEP - 2, NSTEP - 1):
                        b = 6 + n % 2
                        pool.wait_ge(bank[b].full.sem, bank[b].full.at(("o", "s", n), l))
                        alone(pool)
                    norm_params("ln1", ln1_g, ln1_b, l)
                    inverse_roots("ln1", l)
                    pool.wait_ge(h_ready.sem, h_ready.at(("ln1", NT - 1), l))
                    alone(pool)
                    norm_params("ln2", ln2_g, ln2_b, l)
                    pool.wait_ge(zero_land.sem, zero_land.at("all"))
                    alone(pool)
                    pool.wait_ge(slot_ready.sem, slot_ready.at("slot", l))
                    alone(pool)
                    for k in range(2):
                        for t in range(NT):
                            pool.indirect_dma_start(
                                out=x_rows, out_offset=bass.IndirectOffsetOnAxis(ap=slot_keep[:, k, t:t + 1], axis=0),
                                in_=h[:, t, :], in_offset=None).then_inc(scattered.sem, scattered.tick("all", 16))
                    pool.wait_ge(scattered.sem, scattered.at("all", l))
                    alone(pool)
                    load_rows(l, 0, slice(0, C))
                    load_rows(l, 1, slice(C, 2 * C))
                    with pool.Fori(0, NPAIR) as i:
                        book.scope = "pair"
                        pool.wait_ge(bank[1].full.sem, bank[1].full.start(l, i))
                        alone(pool)
                        load_rows(l, 0, bass.ds((i * 2 + 2) * C, C), i)
                        pool.wait_ge(bank[1].full.sem, bank[1].full.at(("pair", "x", 1, 1), l, i))
                        alone(pool)
                        load_rows(l, 1, bass.ds((i * 2 + 3) * C, C), i)
                        for n in range(2):
                            for half in range(2):
                                b = 6 + half
                                pool.wait_ge(bank[b].read, bank[b].full.at(("y", n, half), l, i))
                                alone(pool)
                            pool.dma_start(y_rows[bass.ds((i * 2 + n) * C, C), :], ysb[n]).then_inc(
                                y_stored[n].sem, y_stored[n].tick("y", 16))
                        for n in range(2):
                            pool.wait_ge(y_stored[n].sem, y_stored[n].now(l, i))
                            pool.sem_inc(ysb_free[n].sem, ysb_free[n].tick())
                    book.scope = "tail"
                    for n in range(2):
                        pool.wait_ge(xin_land[n].sem, xin_land[n].now(l))
                        alone(pool)
                    pool.wait_ge(bank[1].full.sem, bank[1].full.at(("pair", "x", 0, 1), l))
                    alone(pool)

                    def over_rows(j, b):
                        pool.dma_start(xin[0], x_rows[bass.ds(j * C + NEXP * C, C), :]).then_inc(
                            over_x.sem, over_x.tick(by=16))
                        pool.wait_ge(over_ye.sem, over_ye.value("over", 1, 0, b))
                        alone(pool)
                        pool.dma_start(y_rows[bass.ds(j * C + NEXP * C, C), :], ysb[0]).then_inc(
                            over_st.sem, over_st.tick(by=16))
                        pool.wait_ge(over_st.sem, over_st.value("over", 16, 0, b))
                        alone(pool)

                    overflow(pool, l, over_rows)
                    for n in range(2):
                        pool.wait_ge(y_stored[n].sem, y_stored[n].now(l))
                        alone(pool)
                    for t in range(NT):
                        if t >= 2:
                            pool.wait_ge(got_used.sem, got_used.at(t - 2, l))
                            alone(pool)
                        for k in range(2):
                            pool.indirect_dma_start(
                                out=got[t % 2][k], out_offset=None, in_=y_rows,
                                in_offset=bass.IndirectOffsetOnAxis(ap=slot_keep[:, k, t:t + 1], axis=0)).then_inc(
                                got_land[t % 2].sem, got_land[t % 2].tick(t, 16))
                    inverse_roots("ln2", l)
                book.scope = "post"
                for t in range(NT):
                    pool.wait_ge(h_ready.sem, h_ready.at(("ln2", t), DEPTH - 1))
                    alone(pool)
                    pool.dma_start(out[0, tok(t), :], h[:, t, :]).then_inc(out_land.sem, out_land.tick(by=16))
                pool.wait_ge(out_land.sem, out_land.now())
                alone(pool)


_INS = ['x', 'positions', 'ln_in_g', 'ln_in_b', 'w_in', 'b_forget', 'diff_lam', 'diff_norm_g', 'w_br', 'w_o', 'ln1_g',
        'ln1_b', 'w_router', 'b_router', 'w_gate', 'w_up', 'w_down', 'ln2_g', 'ln2_b']


def constants():
    i = np.arange(P)
    swap = np.zeros((P, P), np.float32)
    swap[i ^ 32, i] = 1.0
    tri = (i[:, None] < i[None, :]).astype(np.float32)
    e = np.tile(np.arange(NEXP, dtype=np.float32), (P, 1))
    freq = np.float32(10000.0) ** (-np.arange(0, HD, 2, dtype=np.float32) / np.float32(HD))
    inv = freq[i % 32][:, None].astype(np.float32)
    sign = np.where(i % HD < 32, -1.0, 1.0)[:, None].astype(np.float32)
    pick = -np.eye(P, 8, dtype=np.float32)
    cf = np.concatenate([np.eye(P, dtype=np.float32), swap, tri, np.ones((P, P), np.float32), e,
                         np.floor(e / EPG), inv, sign, np.full((P, 1), -0.5, np.float32), pick], 1)
    chunk = np.where(i[None, :] < (i[:, None] // CHUNK + 1) * CHUNK, 0.0, NEG)
    causal = np.where(i[None, :] <= i[:, None], 0.0, NEG)
    cb = np.concatenate([np.eye(P), chunk, causal], 1).astype(mybir.dt.np(BF16))
    lam = [0.8 - 0.6 * math.exp(-0.3 * l) for l in range(DEPTH)]
    cl = np.array([[a, 1.0 - a] for a in lam], np.float32)
    return dict(c_f32=np.ascontiguousarray(cf, np.float32), c_bf16=cb, c_lam=cl)


def kernel(**inputs):
    import concourse.bacc as bacc
    from concourse.bass_utils import run_bass_kernel_spmd as run

    arrays = {f"in_{k}": np.ascontiguousarray(inputs[k]) for k in _INS}
    arrays |= constants()
    book = Book()
    while True:
        nc = bacc.Bacc("TRN2", target_bir_lowering=False, num_devices=1)
        args = [nc.dram_tensor(k, a.shape, mybir.dt.from_np(a.dtype), kind="ExternalInput").ap()
                for k, a in arrays.items()]
        out = nc.dram_tensor("out", (1, T, D), F32, kind="ExternalOutput").ap()
        trunk(nc, book, args, out)
        if book.close():
            break
    r = run(nc, [arrays], core_ids=[0])
    return r.results[0]["out"]
```

```python
import math
from contextlib import ExitStack

import numpy as np
import concourse.bass as bass
from concourse import mybir

ALU = mybir.AluOpType
ACT = mybir.ActivationFunctionType
AX = mybir.AxisListType
F32 = mybir.dt.float32
BF16 = mybir.dt.bfloat16
I32 = mybir.dt.int32
F32R = mybir.dt.float32r
U32 = mybir.dt.uint32

P = 128
T = 512
NT = T // P
D = 1024
KD = D // P
DEPTH = 2
HD = 64
CHUNK = 64
EPS = 1e-5
ALPHA = (2 * DEPTH) ** 0.25
SCALE = HD ** -0.5
NEG = -1e30
TAKEN = -3e38
TOPK = 128
NEXP = 32
NGRP = 4
EPG = NEXP // NGRP
DE = 512
FE = DE // P
BW = 512
KB = BW // P
IDX_H = 4
W_IN = 8012
COL = dict(dq=0, dk=512, dv=1024, sq=1536, sk=2048, sv=2560, iq=3072, ik=3328, iw=3392,
           fq=3396, fk=3908, fv=4420, ff=4932, g=4940)
BRANCHES = ("f", "d", "s")
WBR = dict(d=0, s=1, f=2)
PAIRS = 4
NSTEP = PAIRS * NT
Q_ORDER = (0, 3, 1, 2)

CAP = 80
NOV = (2 * T - 1) // CAP
OVQ = (T - 1) // CAP
NBLK = NEXP + NOV
EPT = 4
NTURN = NEXP // EPT
RING = 4
PIECE = 4096
CROWS = 72
UNIT = PIECE // 4

MAGIC = 12582912.0
PI_LO = 3.1415925
C1, C2 = 6.28125, 0.0019350051879882812
C3 = 2 * math.pi - C1 - C2


class Signal:

    def __init__(self, book, name, sem, turns=NTURN):
        self.book, self.sem, self.turns = book, sem, turns
        self.total = book.totals.setdefault(name, dict(pre=0, layer=0, pair=0, tail=0, post=0, over=0))
        self.marks = book.marks.setdefault(name, {})
        self.n = dict.fromkeys(self.total, 0)
        book.live[name] = self.n

    def tick(self, key=None, by=1):
        s = self.book.scope
        self.n[s] += by
        if key is not None:
            self.marks[key] = (s, self.n[s])
        return by

    def value(self, s, n, l, i):
        c = self.total
        layer = c["layer"] + self.turns * c["pair"] + c["tail"]
        if s == "pre":
            return n
        if s == "over":
            return i * c["over"] + (c["pre"] + n)
        if s == "layer":
            return l * layer + (c["pre"] + n)
        if s == "pair":
            return l * layer + i * c["pair"] + (c["pre"] + c["layer"] + n)
        if s == "tail":
            return l * layer + (c["pre"] + c["layer"] + self.turns * c["pair"] + n)
        return c["pre"] + DEPTH * layer + n

    def at(self, key, l=0, i=NTURN - 1):
        s, n = self.marks.get(key, ("pre", 0))
        return self.value(s, n, l, i)

    def start(self, l=0, i=0):
        return self.value(self.book.scope if self.book.scope == "pair" else "layer", 0, l, i)

    def now(self, l=0, i=NTURN - 1):
        return self.value(self.book.scope, self.n[self.book.scope], l, i)


class Book:
    def __init__(self):
        self.totals, self.marks, self.live, self.where, self.scope = {}, {}, {}, {}, "pre"

    def close(self):
        same = self.totals == self.live
        self.totals, self.live = {k: dict(v) for k, v in self.live.items()}, {}
        return same


class Bank:
    def __init__(self, book, b, tensor, full, read):
        self.t = tensor
        self.full = Signal(book, f"bank{b}", full)
        self.read = read


def trunk(nc, book, ins, out):
    (x, positions, ln_in_g, ln_in_b, w_in, b_forget, diff_lam, diff_norm_g, w_br, w_o, ln1_g, ln1_b,
     w_router, b_router, w_gate, w_up, w_down, ln2_g, ln2_b,
     c_f32, c_bf16, c_lam) = ins
    C = CAP
    x_rows = nc.dram_tensor("x_rows", [NBLK * C, D], F32).ap()
    y_rows = nc.dram_tensor("y_rows", [NBLK * C, D], F32).ap()

    with ExitStack() as ctx:
        def sb(name, shape, dt=F32):
            return ctx.enter_context(nc.sbuf_tensor(name, shape, dt))

        def signal(name, turns=NTURN):
            return Signal(book, name, ctx.enter_context(nc.semaphore(name)), turns)

        ps = ctx.enter_context(nc.psum_tensor("ps", [P, 8, 512], F32))
        bank = [Bank(book, b, ps[:, b, :], ctx.enter_context(nc.semaphore(f"bank{b}_full")),
                     ctx.enter_context(nc.semaphore(f"bank{b}_read"))) for b in range(8)]

        h = sb("h", [P, NT, D])
        hT_hi, hT_lo = sb("hT_hi", [P, KD, T], F32R), sb("hT_lo", [P, KD, T], F32R)
        w_hi, w_lo = sb("w_hi", [P, 2, UNIT], F32R), sb("w_lo", [P, 2, UNIT], F32R)
        ring = sb("ring", [P, RING, PIECE])
        cf = sb("cf", [P, 2 * P + NEXP * 2 + 3])
        cb = sb("cb", [P, 5 * P + 8], BF16)
        ident, perm = (cf[:, i * P:(i + 1) * P] for i in range(2))
        iota_e = cf[:, 2 * P:2 * P + NEXP]
        iota_g = cf[:, 2 * P + NEXP:2 * P + 2 * NEXP]
        c0 = 2 * P + 2 * NEXP
        inv_freq, sign_half, m_half = cf[:, c0:c0 + 1], cf[:, c0 + 1:c0 + 2], cf[:, c0 + 2:c0 + 3]
        pick = cb[0:CROWS, 5 * P:5 * P + 8]
        identb, chunk_mask, causal_mask, tri, ones = (cb[:, i * P:(i + 1) * P] for i in range(5))
        zeros = sb("zeros", [P, NEXP])
        wr_hi, wr_lo = sb("wr_hi", [P, KD, NEXP], F32R), sb("wr_lo", [P, KD, NEXP], F32R)
        br = sb("br", [P, NEXP])
        w_ff = sb("w_ff", [P, KD, 8])
        b_f = sb("b_f", [8, 1])
        lamw = sb("lamw", [P, 8])
        laminit = sb("laminit", [P, 2])
        norm_g = sb("norm_g", [P, P])
        iw = sb("iw", [P, NT, IDX_H])
        small = sb("small", [P, 36])
        stats = sb("stats", [P, NT, 2, 6])
        moments = sb("moments", [P, NT, 2])
        rstd = sb("rstd", [P, NT])

        scr = sb("scr", [P, 18176])
        qT = scr[:, 0:2048].rearrange("p (b t) -> p b t", t=T)
        kT = scr[:, 2048:4096].rearrange("p (b t) -> p b t", t=T)
        v = scr[:, 4096:6144].rearrange("p (b t) -> p b t", t=T)
        yT = scr[:, 6144:10240].rearrange("p (b t) -> p b t", t=T)
        iqT = scr[:, 6144:7168].rearrange("p (b t) -> p b t", t=T)
        ikT = scr[:, 7168:7680]
        oT = scr[:, 10240:12288].rearrange("p (b t) -> p b t", t=T)
        pbuf = scr[:, 12288:14336].rearrange("p (n j k) -> p n j k", n=2, j=2)
        z = [scr[:, 12288:12800], scr[:, 12800:13312]]
        r1, r2 = scr[:, 13312:13824], scr[:, 13824:14336]
        gate = [scr[:, 12288:12800], scr[:, 12800:13312]]
        prod = scr[:, 13312:13824]
        ptb = scr[:, 14336:16384].rearrange("p (n w) -> p n w", n=2)
        wr = scr[:, 14336:14336 + KD * NEXP].rearrange("p (k e) -> p k e", e=NEXP)
        relu = [scr[:, 14336:14848], scr[:, 14848:15360]]
        ffx, ffe = scr[0:8, 15360:15872], scr[0:8, 15872:16384]
        lamv = scr[:, 7680:7936].rearrange("p (a d) -> p a d", d=HD)
        score3 = sb("score3", [P, T])
        score = {1: scr[:, 7936:8192], 2: scr[:, 9216:9600], 3: score3[:, :]}
        zero_row = scr[:, 8192:9216]
        cT, c_rest = scr[0:8, 10240:10752], scr[0:8, 10752:11264]
        c_part = scr[0:8, 11264:11520].bitcast(BF16)
        c_parts = scr[0:CROWS, 9728:9984].bitcast(BF16)
        keep = scr[:, 16384:17152].bitcast(BF16)
        cos, sin = scr[:, 17152:17664], scr[:, 17664:18176]
        onorm = [score3[:, 0:P], score3[:, P:2 * P]]
        ln_g, ln_b = scr[:, 4096:5120], scr[:, 5120:6144]
        xin = [scr[0:C, 0:1024], scr[0:C, 1024:2048]]
        ysb = [scr[0:C, 2048:3072], scr[0:C, 3072:4096]]
        got = [[scr[:, 6144 + (2 * t + k) * 1024:6144 + (2 * t + k + 1) * 1024] for k in range(2)] for t in range(NT)]
        xT = [scr[:, 10240 + n * KD * C:10240 + (n + 1) * KD * C].rearrange("p (k c) -> p k c", c=C) for n in range(2)]
        hid = [scr[:, 11520 + n * 384:11520 + n * 384 + FE * C].rearrange("p (k c) -> p k c", c=C) for n in range(2)]
        act_g = [scr[:, 12288 + n * 512:12288 + n * 512 + FE * C].rearrange("p (k c) -> p k c", c=C) for n in range(2)]
        RT = 14336
        aff = scr[:, RT:RT + 128].rearrange("p (t e) -> p t e", e=NEXP)
        sel = scr[:, RT + 128:RT + 256].rearrange("p (t e) -> p t e", e=NEXP)
        srt = scr[:, RT + 256:RT + 384].rearrange("p (g e) -> p g e", e=EPG)
        gsc = scr[:, RT + 384:RT + 416].rearrange("p (t g) -> p t g", g=8)
        gtop = scr[:, RT + 416:RT + 448].rearrange("p (t g) -> p t g", g=8)
        gidx = scr[:, RT + 448:RT + 480].bitcast(U32).rearrange("p (t g) -> p t g", g=8)
        gidf = scr[:, RT + 480:RT + 484]
        etop = scr[:, RT + 484:RT + 516].rearrange("p (t g) -> p t g", g=8)
        eidx = scr[:, RT + 516:RT + 548].bitcast(U32).rearrange("p (t g) -> p t g", g=8)
        eidf = scr[:, RT + 548:RT + 556].rearrange("p (k t) -> p k t", k=2)
        hot = scr[:, RT + 560:RT + 816].rearrange("p (k t e) -> p k t e", k=2, e=NEXP)
        both = scr[:, RT + 816:RT + 880].bitcast(BF16).rearrange("p (t e) -> p t e", e=NEXP)
        gm = scr[:, RT + 944:RT + 1072].rearrange("p (t e) -> p t e", e=NEXP)
        tmp = scr[:, RT + 1072:RT + 1200].rearrange("p (t e) -> p t e", e=NEXP)
        cum = scr[:, RT + 1200:RT + 1232]
        ovc = scr[:, RT + 1232:RT + 1264]
        base = scr[:, RT + 1264:RT + 1296]
        k8 = [scr[:, RT + 1296 + 8 * i:RT + 1304 + 8 * i].rearrange("p (k t) -> p k t", k=2) for i in range(8)]
        wts, rank, quo, bas, slotf, r8a, r8b, wsum = k8
        slot = scr[:, RT + 1360:RT + 1368].bitcast(U32).rearrange("p (k t) -> p k t", k=2)
        ovt = scr[0:1, RT + 1368:RT + 1368 + NOV * NEXP].rearrange("p (j e) -> p j e", e=NEXP)
        schedf = scr[0:1, RT + 1368 + NOV * NEXP:RT + 1368 + NOV * NEXP + 1 + NOV]
        wts_keep = sb("wts_keep", [P, 2, NT])
        slot_keep = sb("slot_keep", [P, 2, NT], U32)
        sched = sb("sched", [1, 1 + NOV], I32)
        neg_max = [small[:, 0:2], small[:, 2:4]]
        psum_row = [small[:, 4:6], small[:, 6:8]]
        rcp = [small[:, 8:10], small[:, 10:12]]
        rcl = [small[:, 12:13], small[:, 13:14]]
        ssq = [small[:, 14:15], small[:, 15:16]]
        rms = [small[:, 16:17], small[:, 17:18]]
        rms_t = [small[:, 18:19], small[:, 19:20]]
        top8 = small[:, 24:32]
        lameps = small[:, 32:36]
        neg_lam = lamw[:, 0:1]
        gscale = lamw[:, 1:2]

        const_land = signal("const_land")
        idle = ctx.enter_context(nc.semaphore("idle"))
        x_land = signal("x_land")
        pos_land = signal("pos_land")
        zero_land = signal("zero_land")
        small_land = signal("small_land")
        ln_land = signal("ln_land")
        out_land = signal("out_land")
        land = [signal(f"land{s}", NTURN - 1) for s in range(RING)]
        hi_ready = signal("hi_ready")
        lo_ready = signal("lo_ready")
        unit_used = signal("unit_used")
        hT_hi_ready = signal("hT_hi_ready")
        wr_hi_ready = signal("wr_hi_ready")
        wr_ready = signal("wr_ready")
        dve_seq = signal("dve_seq")
        act_seq = signal("act_seq")
        pool_seq = signal("pool_seq")
        moments_ready = signal("moments_ready")
        rstd_ready = signal("rstd_ready")
        h_ready = signal("h_ready")
        angle_ready = signal("angle_ready")
        roped = signal("roped")
        ffe_ready = signal("ffe_ready")
        ffl_ready = signal("ffl_ready")
        lam_prod = signal("lam_prod")
        lam_exp = signal("lam_exp")
        cum_ready = signal("cum_ready")
        keep_ready = signal("keep_ready")
        max_ready = signal("max_ready")
        p_ready = signal("p_ready")
        ssq_ready = signal("ssq_ready")
        rms_ready = signal("rms_ready")
        y_ready = signal("y_ready")
        aff_ready = signal("aff_ready")
        hot_ready = signal("hot_ready")
        slot_ready = signal("slot_ready")
        scattered = signal("scattered")
        xin_land = [signal(f"xin_land{n}") for n in range(2)]
        y_stored = [signal(f"y_stored{n}") for n in range(2)]
        ysb_free = [signal(f"ysb_free{n}") for n in range(2)]
        got_land = [signal(f"got_land{t}") for t in range(NT)]
        got_used = signal("got_used")
        h_scaled = signal("h_scaled")
        sched_ready = signal("sched_ready")
        over_w = signal("over_w")
        over_x = signal("over_x")
        over_t = signal("over_t")
        over_xT = signal("over_xT")
        over_gu = signal("over_gu")
        over_act = signal("over_act")
        over_h = signal("over_h")
        over_y = signal("over_y")
        over_ye = signal("over_ye")
        over_st = signal("over_st")

        pieces = ["idx"]
        for b in BRANCHES:
            pieces += [b + "q", b + "k", b + "v", b + "g0", b + "g1", b + "br"]
        pieces += ["wo0", "wo1"]
        in_slot = {name: n % RING for n, name in enumerate(pieces)}

        def cols(slot, k0=KD):
            return ring[:, slot, :].rearrange("p (k c) -> p k c", k=k0)

        idx_cols = ring[:, in_slot["idx"], 0:KD * 388].rearrange("p (k c) -> p k c", c=388)

        units = [(name, q) for name in pieces if name[1:] != "br" and name[:2] != "wo" for q in range(4)]
        unit_no = {unit: n for n, unit in enumerate(units)}

        def raw_unit(name, q):
            w = cols(in_slot[name])
            if name == "idx":
                return idx_cols[:, :, q * P:min((q + 1) * P, 388)]
            if name[1:] == "v":
                return w[:, 2 * q:2 * q + 2, :]
            return w[:, :, q * P:(q + 1) * P]

        def unit_part(part, name, q):
            k, c = raw_unit(name, q).shape[1:]
            return part[:, unit_no[name, q] % 2, 0:k * c].rearrange("p (k c) -> p k c", c=c)

        def unit_end(name, q):
            if name == "idx":
                return ("iq0", "iq1", "ik", "iw")[q]
            if name[1:] == "v" and q < 3:
                return None
            if name[1] == "g":
                return ("g", name[0], 4 * int(name[2]) + q)
            return (name, q)

        def wait_unit_used(eng, name, q, l):
            key = unit_end(name, q)
            if key is None:
                eng.wait_ge(unit_used.sem, unit_used.at((name, q), l))
            else:
                b = book.where.get(key, 0)
                eng.wait_ge(bank[b].full.sem, bank[b].full.at(key, l))

        last_reader = {"wo0": ("m", NT - 1, 1), "wo1": ("m", NT - 1, 1)}
        for b in BRANCHES:
            last_reader[b + "br"] = ("br", b, KD - 1)

        def expert_slot(e, m):
            return (3 * e + m + 1) % RING

        def width(t):
            return (t + 1) * P

        def tile_of(n):
            return Q_ORDER[n % NT]

        def tok(t):
            return slice(t * P, (t + 1) * P)

        with nc.Block() as block:

            def over_load(sp, one, j, b):
                sp.wait_ge(over_y.sem, over_y.value("over", 0, 0, b))
                alone(sp)
                e = sp.value_load(sched[0:1, bass.ds(j + 1, 1)], min_val=0, max_val=NEXP - 1)
                for s, w in enumerate((w_gate, w_up, w_down)):
                    src = w[one, bass.ds(e, 1)].rearrange("o q (k p) c -> p (o q k) c", p=P)
                    sp.dma_start(cols(s, FE if s == 2 else KD), src).then_inc(over_w.sem, over_w.tick(by=16))
                sp.wait_ge(over_y.sem, over_y.value("over", 1, 0, b))
                alone(sp)

            def alone(eng):
                eng.sem_inc(idle, 1)

            blocks_before = {}

            def count_blocks(eng):
                blocks_before[eng.engine] = eng.alloc_register("blocks_before_" + eng.engine.name)
                eng.reg_mov(blocks_before[eng.engine], 0)

            def overflow(eng, l, body):
                eng.wait_ge(sched_ready.sem, sched_ready.at("sched", l))
                alone(eng)
                n_over = eng.value_load(sched[0:1, 0:1], min_val=0, max_val=NOV)
                before = eng.snap(blocks_before[eng.engine], min_val=0, max_val=NOV * DEPTH)
                with eng.If(n_over > 0):
                    with eng.Fori(0, NOV) as j:
                        with eng.If(j < n_over):
                            book.scope = "over"
                            body(j, before + j)
                book.scope = "tail"
                eng.reg_add(blocks_before[eng.engine], blocks_before[eng.engine], n_over)

            @block.sync
            def _(sp):
                book.scope = "pre"
                sp.dma_start(r1.bitcast(I32), positions[0].partition_broadcast(P)).then_inc(
                    pos_land.sem, pos_land.tick("all", 16))
                sp.dma_start(cf[:, :], c_f32).then_inc(pos_land.sem, pos_land.tick("all", 16))
                sp.dma_start(h[:, :, :], x[0].rearrange("(t p) d -> p t d", p=P)).then_inc(
                    x_land.sem, x_land.tick("all", 16))
                for src, dst in ((c_bf16, cb[:, :]),
                                 (w_router.rearrange("(k p) e -> p k e", p=P), wr),
                                 (b_router.partition_broadcast(P), br[:, :]),
                                 (ln_in_g.partition_broadcast(P), ln_g),
                                 (ln_in_b.partition_broadcast(P), ln_b)):
                    sp.dma_start(dst, src).then_inc(const_land.sem, const_land.tick("all", 16))

                count_blocks(sp)
                with sp.Fori(0, DEPTH) as l:
                    book.scope = "layer"
                    one = bass.ds(l, 1)

                    def multiplied(key, i=NTURN - 1):
                        b = book.where.get(key, 0)
                        sp.wait_ge(bank[b].full.sem, bank[b].full.at(key, l, i))
                        alone(sp)

                    def released(name):
                        if name in last_reader:
                            multiplied(last_reader[name])
                        else:
                            sp.wait_ge(lo_ready.sem, lo_ready.at((name, 3), l))
                            alone(sp)

                    for n, name in enumerate(pieces):
                        s = in_slot[name]
                        if n == RING:
                            sp.wait_ge(h_ready.sem, h_ready.start(l))
                            alone(sp)
                            for src, dst in (
                                    (w_in[one, :, COL["ff"]:COL["ff"] + 8].rearrange("o (k p) c -> p (o k) c", p=P), w_ff[:, :, :]),
                                    (b_forget[one, :].rearrange("o c -> c o"), b_f[:, :]),
                                    (diff_lam[one].rearrange("o a d -> (o a d)").partition_broadcast(P),
                                     lamv[:, :, :].rearrange("p a d -> p (a d)")),
                                    (c_lam[one, :].rearrange("o c -> (o c)").partition_broadcast(P), laminit[:, :]),
                                    (diff_norm_g[one, :].rearrange("o c -> (o c)").partition_broadcast(P), norm_g[:, :])):
                                sp.dma_start(dst, src).then_inc(small_land.sem, small_land.tick("all", 16))
                        if n >= RING:
                            released(pieces[n - RING])
                        if name == "idx":
                            parts = [(w_in[one, :, COL["iq"]:COL["iw"]].rearrange("o (k p) c -> p (o k) c", p=P),
                                      idx_cols[:, :, 0:320]),
                                     (w_in[one, :, COL["ik"]:COL["fq"]].rearrange("o (k p) c -> p (o k) c", p=P),
                                      idx_cols[:, :, 320:388])]
                        elif name[1:] == "br":
                            parts = [(w_br[one, WBR[name[0]]].rearrange("o (k p) c -> p (o k) c", p=P), cols(s, KB))]
                        elif name[:2] == "wo":
                            r0 = int(name[2]) * BW
                            parts = [(w_o[one, r0:r0 + BW, :].rearrange("o (k p) c -> p (o k) c", p=P), cols(s, KB))]
                        else:
                            c = COL[name] if name in COL else COL["g"] + WBR[name[0]] * D + int(name[2]) * BW
                            parts = [(w_in[one, :, c:c + BW].rearrange("o (k p) c -> p (o k) c", p=P), cols(s))]
                        for src, dst in parts:
                            sp.dma_start(dst, src).then_inc(land[s].sem, land[s].tick(name, 16))

                    def expert_piece(n, key, e):
                        s, m = expert_slot(n // 3, n % 3), n % 3
                        src = (w_gate, w_up, w_down)[m][one, e].rearrange("o q (k p) c -> p (o q k) c", p=P)
                        sp.dma_start(cols(s, FE if m == 2 else KD), src).then_inc(land[s].sem, land[s].tick(key, 16))

                    def used(n, i=NTURN - 1):
                        multiplied(("y", n // 3, 1) if n % 3 == 2 else ("gu", n // 3, n % 3), i)

                    for n in range(RING):
                        released([p_ for p_ in pieces if in_slot[p_] == expert_slot(n // 3, n % 3)][-1])
                        expert_piece(n, ("first", n), slice(n // 3, n // 3 + 1))
                    with sp.Fori(0, NTURN - 1) as i:
                        book.scope = "pair"
                        for n in range(3 * EPT):
                            used(n, i)
                            after = n + RING
                            expert_piece(after % (3 * EPT), None, bass.ds(i * EPT + after // 3, 1))
                    book.scope = "tail"
                    for n in range(3 * EPT - RING):
                        used(n)
                        after = n + RING
                        e = (NTURN - 1) * EPT + after // 3
                        expert_piece(after, None, slice(e, e + 1))
                    multiplied(("y", EPT - 1, 1))
                    overflow(sp, l, lambda j, b: over_load(sp, one, j, b))
                    sp.wait_ge(got_used.sem, got_used.at(0, l))
                    alone(sp)

            @block.tensor
            def _(pe):
                mm = nc.tensor.matmul
                turn = {"pj": 0, "rope": 0}
                rope_src = {}

                def free(b, l=0, i=0):
                    pe.wait_ge(bank[b].read, bank[b].full.now(l, i))

                def filled(ins, b, key):
                    book.where[key] = b
                    ins.then_inc(bank[b].full.sem, bank[b].full.tick(key))

                def in_sbuf(b, key, l=0, i=NTURN - 1):
                    pe.wait_ge(bank[b].read, bank[b].full.at(key, l, i))

                def transpose_tile(key, t, l=0):
                    pe.wait_ge(h_ready.sem, h_ready.at((key, t), l))
                    for half in range(2):
                        b = 2 * (t % 2) + half
                        free(b, l)
                        for k in range(4):
                            kd = 4 * half + k
                            ins = nc.tensor.transpose(bank[b].t[:, k * P:(k + 1) * P],
                                                      h[:, t, kd * P:(kd + 1) * P], ident)
                        filled(ins, b, (key, t, half))

                def transpose_h(key, l=0):
                    for t in range(NT):
                        transpose_tile(key, t, l)

                def split_product(out, a, b, first, last):
                    mm(out, a[0], b[1], start=first, stop=False)
                    mm(out, a[1], b[0], start=False, stop=False)
                    return mm(out, a[0], b[0], start=False, stop=last)

                def unit(name, q, l):
                    pe.wait_ge(lo_ready.sem, lo_ready.at((name, q), l))
                    parts = [unit_part(part, name, q) for part in (w_hi, w_lo)]
                    return lambda k, c=slice(None): [part[:, k, c] for part in parts]

                def hT(k, c=slice(None)):
                    return hT_hi[:, k, c], hT_lo[:, k, c]

                def project(key, l, name, q, b=None):
                    if b is None:
                        b = turn["pj"] % 4
                        turn["pj"] += 1
                    w = unit(name, q, l)
                    free(b, l)
                    for k in range(KD):
                        ins = split_product(bank[b].t, w(k), hT(k), k == 0, k == KD - 1)
                    filled(ins, b, key)

                def turn_halves(l, r):
                    b = 4 + r % 2
                    zb, zkey = rope_src[r]
                    in_sbuf(zb, zkey, l)
                    free(b, l)
                    filled(mm(bank[b].t, perm, z[r % 2], start=True, stop=True), b, ("rope", r))

                def roped_blocks(keys, l, name):
                    for n, key in enumerate(keys):
                        project(key, l, name, n)
                        r = turn["rope"]
                        turn["rope"] += 1
                        rope_src[r] = (book.where[key], key)
                        if n:
                            turn_halves(l, r - 1)
                    turn_halves(l, turn["rope"] - 1)

                def landed(name, l):
                    s = in_slot[name]
                    pe.wait_ge(land[s].sem, land[s].at(name, l))

                def index_logits(l):
                    roped_blocks(["iq0", "iq1", "ik"], l, "idx")
                    w = unit("idx", 3, l)
                    b = turn["pj"] % 4
                    turn["pj"] += 1
                    free(b, l)
                    for t in range(NT):
                        for k in range(KD):
                            ins = split_product(bank[b].t[:, t * IDX_H:(t + 1) * IDX_H], hT(k, tok(t)), w(k),
                                                k == 0, k == KD - 1)
                    filled(ins, b, "iw")
                    pe.wait_ge(roped.sem, roped.at("ik", l))
                    for t in range(1, NT):
                        for hd in range(IDX_H):
                            free(hd, l)
                            rows = slice(HD * (hd % 2), HD * (hd % 2) + HD)
                            ins = mm(bank[hd].t[:, 0:width(t)], iqT[rows, hd // 2, tok(t)],
                                     ikT[rows, 0:width(t)], start=True, stop=True)
                            filled(ins, hd, ("logit", t, hd))
                    turn["pj"] = 0

                def forget_logits(l):
                    pe.wait_ge(small_land.sem, small_land.at("all", l))
                    b = turn["pj"] % 4
                    turn["pj"] += 1
                    free(b, l)
                    for k in range(KD):
                        for part, x_part in enumerate(hT(k)):
                            ins = mm(bank[b].t[0:8, :], w_ff[:, k, :], x_part.bitcast(F32), start=k + part == 0,
                                     stop=k + part == KD)
                    filled(ins, b, "ff")

                def queries_keys_values(br, l):
                    for what in "qk":
                        name = br + what
                        if br == "f":
                            for n in range(KB):
                                project((name, n), l, name, n)
                        else:
                            roped_blocks([(name, n) for n in range(KB)], l, name)
                    name = br + "v"
                    first = turn["pj"]
                    turn["pj"] += NT
                    for q in range(4):
                        w = unit(name, q, l)
                        for t in range(NT):
                            b = (first + t) % 4
                            if q == 0:
                                free(b, l)
                            for k in range(2):
                                ins = split_product(bank[b].t, hT(2 * q + k, tok(t)), w(k), q + k == 0, q + k == 4)
                            if q == 3:
                                filled(ins, b, (name, t))
                        if q < 3:
                            ins.then_inc(unit_used.sem, unit_used.tick((name, q)))

                def attention(br, l):
                    if br == "f":
                        pe.wait_ge(cum_ready.sem, cum_ready.at("cum", l))
                        for t in range(NT):
                            for what in "qk":
                                in_sbuf(book.where[(br + what, t)], (br + what, t), l)
                    else:
                        pe.wait_ge(roped.sem, roped.at((br + "k", KB - 1), l))
                    if br == "s":
                        pe.wait_ge(keep_ready.sem, keep_ready.at("keep", l))
                    for t in range(NT):
                        in_sbuf(book.where[(br + "v", t)], (br + "v", t), l)

                    def scores(n):
                        p, t = n // NT, tile_of(n)
                        W = width(t)
                        for j in range(2):
                            b = 2 * (n % 2) + j
                            rows = slice(HD * j, HD * j + HD)
                            free(b, l)
                            o = bank[b].t
                            part = br != "s" or t == 0
                            mm(o[:, 0:W], qT[rows, p, tok(t)], kT[rows, p, 0:W], start=True,
                               stop=part and br != "f")
                            if br == "f":
                                mm(o[:, 0:W], pick[:, 2 * p + j:2 * p + j + 1].to_broadcast([CROWS, P]), c_parts[:, 0:W], start=False, stop=True)
                            if not part:
                                ins = mm(o[:, 0:W], identb, keep[:, (t - 1) * T:(t - 1) * T + W], start=False,
                                         stop=True)
                            else:
                                ins = mm(o[:, t * P:W], identb, causal_mask if br == "f" else chunk_mask,
                                         start=False, stop=True, skip_group_check=True)
                            filled(ins, b, ("score", br, n, j))

                    def turn_probs(n):
                        t = tile_of(n)
                        pe.wait_ge(p_ready.sem, p_ready.at((br, n), l))
                        for j in range(1 if br == "d" else 2):
                            b = 4 + (n % 2 if br == "d" else j)
                            free(b, l)
                            for k in range(t + 1):
                                ins = nc.tensor.transpose(bank[b].t[:, k * P:(k + 1) * P],
                                                          pbuf[:, n % 2, j, k * P:(k + 1) * P], ident)
                            filled(ins, b, ("pt", br, n, j))

                    def values(n):
                        p, t = n // NT, tile_of(n)
                        b = 6 + n % 2
                        free(b, l)
                        if br == "d":
                            in_sbuf(4 + n % 2, ("pt", br, n, 0), l)
                            for k in range(t + 1):
                                ins = mm(bank[b].t[:, 0:P], ptb[:, n % 2, k * P:(k + 1) * P], v[:, k, tok(p)],
                                         start=(k == 0), stop=(k == t))
                        else:
                            for j in range(2):
                                in_sbuf(4 + j, ("pt", br, n, j), l)
                                for k in range(t + 1):
                                    ins = mm(bank[b].t[j * HD:(j + 1) * HD, 0:P],
                                             v[:, k, (2 * p + j) * HD:(2 * p + j + 1) * HD],
                                             ptb[:, n % 2, j * 512 + k * P:j * 512 + (k + 1) * P],
                                             start=(k == 0), stop=(k == t))
                        filled(ins, b, ("o", br, n))

                    def turn_normed(n):
                        b = 6 + n % 2
                        free(b, l)
                        filled(nc.tensor.transpose(bank[b].t[:, 0:P], onorm[n % 2], ident), b, ("on", n))

                    for n in range(NSTEP + 4):
                        if n < NSTEP:
                            scores(n)
                        if 2 <= n < NSTEP + 2:
                            turn_probs(n - 2)
                        if 3 <= n < NSTEP + 3:
                            values(n - 3)
                        if br == "d" and n >= 4:
                            turn_normed(n - 4)

                def gated_output(br, l):
                    for n in (NSTEP - 2, NSTEP - 1):
                        b = 6 + n % 2
                        in_sbuf(b, ("on", n) if br == "d" else ("o", br, n), l)
                    landed(br + "br", l)
                    wb = cols(in_slot[br + "br"], KB)
                    for c in range(KD):
                        b = c % 2
                        project(("g", br, c), l, br + "g" + str(c // 4), c % 4, b)
                        free(2 + b, l)
                        for k in range(KB):
                            ins = mm(bank[2 + b].t, wb[:, k, c * P:(c + 1) * P], oT[:, k, :], start=(k == 0),
                                     stop=(k == KB - 1))
                        filled(ins, 2 + b, ("br", br, c))

                def output(l):
                    pe.wait_ge(y_ready.sem, y_ready.at("y", l))
                    landed("wo0", l)
                    landed("wo1", l)
                    for t in range(NT):
                        for half in range(2):
                            b = 4 + (2 * t + half) % 4
                            free(b, l)
                            for k in range(KD):
                                w = cols(in_slot["wo0" if k < KB else "wo1"], KB)
                                ins = mm(bank[b].t, yT[:, k, tok(t)], w[:, k % KB, half * 512:(half + 1) * 512],
                                         start=(k == 0), stop=(k == KD - 1))
                            filled(ins, b, ("m", t, half))
                        if t:
                            transpose_tile("ln1", t - 1, l)
                    transpose_tile("ln1", NT - 1, l)

                def transposed(key, l):
                    for t in (NT - 2, NT - 1):
                        for half in range(2):
                            in_sbuf(2 * (t % 2) + half, (key, t, half), l)

                def route(l):
                    transposed("ln1", l)
                    free(4, l)
                    for t in range(NT):
                        for k in range(KD):
                            ins = split_product(bank[4].t[:, t * NEXP:(t + 1) * NEXP], hT(k, tok(t)),
                                                (wr_hi[:, k, :], wr_lo[:, k, :]), k == 0, k == KD - 1)
                    filled(ins, 4, "router")
                    pe.wait_ge(hot_ready.sem, hot_ready.at("hot", l))
                    free(5, l)
                    for t in range(NT + 1):
                        for u in range(min(t + 1, NT)):
                            ins = mm(bank[5].t[:, t * NEXP:(t + 1) * NEXP], tri if u == t else ones, both[:, u, :],
                                     start=(u == 0), stop=(u == min(t, NT - 1)))
                    filled(ins, 5, "rank")

                def turn_rows(n, b0, fill):
                    for half in range(2):
                        for k in range(4):
                            kd = 4 * half + k
                            ins = nc.tensor.transpose(bank[b0 + half].t[:, k * C:(k + 1) * C],
                                                      xin[n][:, kd * P:(kd + 1) * P], ident[0:C, 0:C])
                        fill(ins, half)

                def up(n, s, bnk, fill):
                    w = cols(s)
                    for f in range(FE):
                        for k in range(KD):
                            ins = mm(bank[bnk].t[:, f * C:(f + 1) * C], w[:, k, f * P:(f + 1) * P], xT[n][:, k, :],
                                     start=(k == 0), stop=(k == KD - 1))
                    fill(ins)

                def down(n, s, half, bnk):
                    w = cols(s, FE)
                    for f in range(FE):
                        ins = mm(bank[bnk].t[0:C, :], hid[n][:, f, :], w[:, f, half * 512:(half + 1) * 512],
                                 start=(f == 0), stop=(f == FE - 1))
                    return ins

                def expert_rows(e, landed_at, l, i=0):
                    n = e % 2
                    pe.wait_ge(xin_land[n].sem, landed_at)
                    free(0, l, i)
                    free(1, l, i)
                    turn_rows(n, 0, lambda ins, half: filled(ins, half, ("x", e, half)))

                def expert_turn(l, i):
                    def piece_landed(e, m):
                        s = expert_slot(e, m)
                        first = (s - 1) % RING
                        pe.wait_ge(land[s].sem, land[s].at(("first", first), l) + i * land[s].total["pair"]
                                   + 16 * ((3 * e + m) // RING))
                        return s

                    for e in range(EPT):
                        n = e % 2
                        free(0, l, i)
                        free(1, l, i)
                        for m in range(2):
                            s, b = piece_landed(e, m), 2 + 2 * n + m
                            free(b, l, i)
                            up(n, s, b, lambda ins: filled(ins, b, ("gu", e, m)))
                        expert_rows(e + 1, xin_land[(e + 1) % 2].start(l, i) + 16 * ((e + 1) // 2), l, i)
                        s = piece_landed(e, 2)
                        in_sbuf(3 + 2 * n, ("gu", e, 1), l, i)
                        for half in range(2):
                            free(6 + half, l, i)
                            filled(down(n, s, half, 6 + half), 6 + half, ("y", e, half))

                def over_block(l, j, b):
                    pe.wait_ge(over_x.sem, over_x.value("over", 16, 0, b))
                    for half in range(2):
                        for k in range(4):
                            kd = 4 * half + k
                            ins = nc.tensor.transpose(bank[half].t[:, k * C:(k + 1) * C],
                                                      xin[0][:, kd * P:(kd + 1) * P], ident[0:C, 0:C])
                    ins.then_inc(over_t.sem, over_t.tick())
                    pe.wait_ge(over_w.sem, over_w.value("over", 48, 0, b))
                    pe.wait_ge(over_xT.sem, over_xT.value("over", 1, 0, b))
                    up(0, 0, 2, lambda ins: None)
                    up(0, 1, 3, lambda ins: ins.then_inc(over_gu.sem, over_gu.tick()))
                    pe.wait_ge(over_h.sem, over_h.value("over", 1, 0, b))
                    down(0, 2, 0, 6)
                    down(0, 2, 1, 7).then_inc(over_y.sem, over_y.tick())
                    pe.wait_ge(over_ye.sem, over_ye.value("over", 1, 0, b))

                book.scope = "pre"
                pe.wait_ge(const_land.sem, const_land.at("all"))
                transpose_h("ln0")
                pe.wait_ge(wr_ready.sem, wr_ready.at("wr"))
                for b in range(4, 8):
                    pe.sem_inc(bank[b].full.sem, bank[b].full.tick())
                    pe.sem_inc(bank[b].read, 1)
                pe.sem_inc(over_y.sem, over_y.tick())
                count_blocks(pe)
                with pe.Fori(0, DEPTH) as l:
                    book.scope = "layer"
                    for b in range(4):
                        pe.wait_ge(bank[b].read, bank[b].full.now(l))
                    index_logits(l)
                    forget_logits(l)
                    for br_ in BRANCHES:
                        queries_keys_values(br_, l)
                        attention(br_, l)
                        gated_output(br_, l)
                        turn["pj"] = 0
                    output(l)
                    route(l)
                    expert_rows(0, xin_land[0].start(l) + 16, l)
                    with pe.Fori(0, NTURN) as i:
                        book.scope = "pair"
                        expert_turn(l, i)
                    book.scope = "tail"
                    for b in range(8):
                        pe.wait_ge(bank[b].read, bank[b].full.now(l))
                    overflow(pe, l, lambda j, b: over_block(l, j, b))
                    transpose_h("ln2", l)

            @block.scalar
            def _(act):
                rope_n = [0]
                split = [0]

                def filled(b, key, l=0, i=NTURN - 1):
                    act.wait_ge(bank[b].full.sem, bank[b].full.at(key, l, i))

                def in_sbuf(b, key, l=0, i=NTURN - 1):
                    act.wait_ge(bank[b].read, bank[b].full.at(key, l, i))

                def copy(dst, b, src, scale=1.0):
                    nc.scalar.activation(dst, src, ACT.Copy, scale=scale).then_inc(bank[b].read, 1)

                def take_hT(key, l=0):
                    for t in range(NT):
                        for half in range(2):
                            b = 2 * (t % 2) + half
                            filled(b, (key, t, half), l)
                            nc.scalar.activation(hT_hi[:, 4 * half:4 * half + 4, tok(t)], bank[b].t.rearrange(
                                "p (k c) -> p k c", c=P), ACT.Copy).then_inc(hT_hi_ready.sem,
                                                                            hT_hi_ready.tick((key, t, half)))

                def split_to(last, l):
                    while split[0] <= unit_no[last]:
                        name, q = units[split[0]]
                        s = in_slot[name]
                        act.wait_ge(land[s].sem, land[s].at(name, l))
                        if split[0] >= 2:
                            wait_unit_used(act, *units[split[0] - 2], l)
                        nc.scalar.activation(unit_part(w_hi, name, q), raw_unit(name, q), ACT.Copy).then_inc(
                            hi_ready.sem, hi_ready.tick((name, q)))
                        split[0] += 1

                def take_z(key, l, scale=1.0, after=None):
                    r = rope_n[0]
                    rope_n[0] += 1
                    b = book.where.get(key, 0)
                    filled(b, key, l)
                    if r >= 2:
                        act.wait_ge(roped.sem, roped.at(("n", r - 2), l))
                    copy(z[r % 2], b, bank[b].t, scale)

                def take_projections(br, l):
                    if br != "f":
                        for c in (KD - 2, KD - 1):
                            before = BRANCHES[BRANCHES.index(br) - 1]
                            in_sbuf(2 + c % 2, ("br", before, c), l)
                    for what in "qk":
                        for n in range(KB):
                            key = (br + what, n)
                            split_to(units[unit_no[key] + 1], l)
                            sc = SCALE if what == "q" else 1.0
                            if br == "f":
                                b = book.where.get(key, 0)
                                filled(b, key, l)
                                copy((qT if what == "q" else kT)[:, n, :], b, bank[b].t, sc)
                            else:
                                take_z(key, l, sc)
                    split_to((br + "v", 3), l)
                    for t in range(NT):
                        b = book.where.get((br + "v", t), 0)
                        filled(b, (br + "v", t), l)
                        copy(v[:, t, :], b, bank[b].t)
                    split_to((br + "g0", 1), l)

                def attention(br, l):
                    for n in range(NSTEP + 4):
                        if n < NSTEP:
                            W = width(tile_of(n))
                            act.wait_ge(max_ready.sem, max_ready.at((br, n), l))
                            if n >= 2:
                                for j in range(1 if br == "d" else 2):
                                    filled(4 + (n % 2 if br == "d" else j), ("pt", br, n - 2, j), l)
                            for j in range(2):
                                b = 2 * (n % 2) + j
                                nc.scalar.activation(pbuf[:, n % 2, j, 0:W], bank[b].t[:, 0:W], ACT.Exp,
                                                     bias=neg_max[n % 2][:, j:j + 1],
                                                     accum_out=psum_row[n % 2][:, j:j + 1]).then_inc(bank[b].read, 1)
                        if 2 <= n < NSTEP + 2:
                            m = n - 2
                            b = 4 + (m % 2 if br == "d" else 0)
                            filled(b, ("pt", br, m, 0), l)
                            if m >= 2:
                                filled(6 + m % 2, ("o", br, m - 2), l)
                            copy(ptb[:, m % 2, 0:width(tile_of(m))], b, bank[b].t[:, 0:width(tile_of(m))])
                        if 3 <= n < NSTEP + 3:
                            m = n - 3
                            b = 6 + m % 2
                            filled(b, ("o", br, m), l)
                            if br == "d":
                                nc.scalar.activation(bank[b].t[:, P:2 * P], bank[b].t[:, 0:P], ACT.Square,
                                                     accum_out=ssq[m % 2]).then_inc(ssq_ready.sem, ssq_ready.tick(m))
                            else:
                                copy(oT[:, m // NT, tok(tile_of(m))], b, bank[b].t[:, 0:P])
                        if br == "d" and n >= 4:
                            m = n - 4
                            b = 6 + m % 2
                            filled(b, ("on", m), l)
                            copy(oT[:, m // NT, tok(tile_of(m))], b, bank[b].t[:, 0:P])

                def gates(br, l):
                    first = unit_no[br + "g0", 0]
                    for c in range(KD):
                        b = c % 2
                        split_to(units[min(first + c + 1, len(units) - 1)], l)
                        filled(b, ("g", br, c), l)
                        if c >= 2:
                            in_sbuf(2 + b, ("br", br, c - 2), l)
                        nc.scalar.activation(gate[b], bank[b].t, ACT.Sigmoid).then_inc(bank[b].read, 1)
                    split_to(units[min(first + KD + 1, len(units) - 1)], l)

                book.scope = "pre"
                act.wait_ge(angle_ready.sem, angle_ready.at("angles"))
                nc.scalar.activation(sin, z[0], ACT.Sin).then_inc(act_seq.sem, act_seq.tick())
                nc.scalar.activation(cos, z[1], ACT.Sin).then_inc(act_seq.sem, act_seq.tick("trig"))
                take_hT("ln0")
                act.wait_ge(const_land.sem, const_land.at("all"))
                nc.scalar.activation(wr_hi[:, :, :], wr, ACT.Copy).then_inc(wr_hi_ready.sem, wr_hi_ready.tick("wr"))
                count_blocks(act)
                with act.Fori(0, DEPTH) as l:
                    book.scope = "layer"
                    rope_n[0] = 0
                    act.wait_ge(h_ready.sem, h_ready.start(l))
                    act.wait_ge(dve_seq.sem, dve_seq.at("trig"))
                    split[0] = 0
                    for n, key in enumerate(("iq0", "iq1", "ik")):
                        split_to(("idx", n + 1), l)
                        take_z(key, l)
                    split_to(("fq", 1), l)
                    m = 0
                    for t in range(1, NT):
                        for hd in range(IDX_H):
                            filled(hd, ("logit", t, hd), l)
                            if m >= 2:
                                act.wait_ge(dve_seq.sem, dve_seq.at(("weighed", m - 2), l))
                            nc.scalar.activation(relu[m % 2][:, 0:width(t)], bank[hd].t[:, 0:width(t)],
                                                 ACT.Relu).then_inc(bank[hd].read, 1)
                            m += 1
                    act.wait_ge(lam_prod.sem, lam_prod.at("lam", l))
                    nc.scalar.activation(lamw[:, 4:6], lamw[:, 2:4], ACT.Exp).then_inc(lam_exp.sem, lam_exp.tick("lam"))
                    act.wait_ge(ffe_ready.sem, ffe_ready.at("ffe", l))
                    nc.scalar.activation(ffe, ffe, ACT.Exp).then_inc(act_seq.sem, act_seq.tick())
                    act.wait_ge(act_seq.sem, act_seq.now(l))
                    nc.scalar.activation(ffe, ffe, ACT.Ln, bias=1.0).then_inc(ffl_ready.sem, ffl_ready.tick("ffl"))
                    for br_ in BRANCHES:
                        take_projections(br_, l)
                        attention(br_, l)
                        gates(br_, l)
                    take_hT("ln1", l)
                    filled(4, "router", l)
                    nc.scalar.activation(aff, bank[4].t[:, 0:P].rearrange("p (t e) -> p t e", e=NEXP),
                                         ACT.Sigmoid).then_inc(bank[4].read, 1)

                    def rows(e, i=0):
                        n = e % 2
                        filled(0, ("x", e, 0), l, i)
                        copy(xT[n][:, 0:4, :], 0, bank[0].t[:, 0:4 * C].rearrange("p (k c) -> p k c", c=C))

                    rows(0)
                    act.wait_ge(scattered.sem, scattered.at("all", l))
                    nc.scalar.activation(h[:, :, :], h[:, :, :], ACT.Copy, scale=ALPHA).then_inc(
                        h_scaled.sem, h_scaled.tick("h"))
                    with act.Fori(0, NTURN) as i:
                        book.scope = "pair"


                        def silu(e):
                            n = e % 2
                            b = 2 + 2 * n
                            filled(b, ("gu", e, 0), l, i)
                            nc.scalar.activation(act_g[n], bank[b].t[:, 0:FE * C].rearrange("p (k c) -> p k c", c=C),
                                                 ACT.Silu).then_inc(bank[b].read, 1)

                        def y_half(e):
                            n = e % 2
                            filled(6, ("y", e, 0), l, i)
                            if e < 2:
                                act.wait_ge(ysb_free[n].sem, ysb_free[n].start(l, i))
                            else:
                                act.wait_ge(y_stored[n].sem, y_stored[n].start(l, i) + 16)
                            copy(ysb[n][:, 0:512], 6, bank[6].t[0:C, :])

                        for e in range(EPT):
                            silu(e)
                            rows(e + 1, i)
                            y_half(e)
                    book.scope = "tail"

                    def over_silu(j, b):
                        act.wait_ge(over_gu.sem, over_gu.value("over", 1, 0, b))
                        nc.scalar.activation(act_g[0], bank[2].t[:, 0:FE * C].rearrange("p (k c) -> p k c", c=C),
                                             ACT.Silu).then_inc(over_act.sem, over_act.tick())

                    overflow(act, l, over_silu)
                    take_hT("ln2", l)

            @block.vector
            def _(dve):
                V = nc.vector
                split = [0]

                def link(ins, l=0, i=NTURN - 1, key=None):
                    ins.then_inc(dve_seq.sem, dve_seq.tick(key))
                    dve.wait_ge(dve_seq.sem, dve_seq.now(l, i))

                def filled(b, key, l=0, i=NTURN - 1):
                    dve.wait_ge(bank[b].full.sem, bank[b].full.at(key, l, i))

                def in_sbuf(b, key, l=0, i=NTURN - 1):
                    dve.wait_ge(bank[b].read, bank[b].full.at(key, l, i))

                def split_to(last, l):
                    while split[0] <= unit_no[last]:
                        name, q = units[split[0]]
                        dve.wait_ge(hi_ready.sem, hi_ready.at((name, q), l))
                        V.tensor_tensor(unit_part(w_lo, name, q), raw_unit(name, q),
                                        unit_part(w_hi, name, q).bitcast(F32), ALU.subtract).then_inc(
                            lo_ready.sem, lo_ready.tick((name, q)))
                        split[0] += 1

                def take_hT(key, t, l):
                    for half in range(2):
                        b = 2 * (t % 2) + half
                        dst = slice(4 * half, 4 * half + 4), tok(t)
                        dve.wait_ge(hT_hi_ready.sem, hT_hi_ready.at((key, t, half), l))
                        V.tensor_tensor(hT_lo[:, dst[0], dst[1]], bank[b].t.rearrange("p (k c) -> p k c", c=P),
                                        hT_hi[:, dst[0], dst[1]].bitcast(F32), ALU.subtract).then_inc(bank[b].read, 1)

                def layer_norm(key, l, source):
                    def moments_of(t):
                        source(t)
                        for half in range(2):
                            ins = V.bn_stats(stats[:, t, half, :], h[:, t, half * 512:(half + 1) * 512])
                            ins.then_inc(dve_seq.sem, dve_seq.tick())
                        dve.wait_ge(dve_seq.sem, dve_seq.now(l))
                        alone(dve)
                        V.bn_aggr(moments[:, t, :], stats[:, t, :, :]).then_inc(
                            moments_ready.sem, moments_ready.tick((key, t)))

                    def normalise(t):
                        if t == 0 and key != "ln0":
                            dve.wait_ge(ln_land.sem, ln_land.at(key, l))
                        dve.wait_ge(rstd_ready.sem, rstd_ready.at((key, t), l))
                        link(V.scalar_tensor_tensor(h[:, t, :], h[:, t, :], moments[:, t, 0:1], ln_g,
                                                    ALU.subtract, ALU.mult), l)
                        V.scalar_tensor_tensor(h[:, t, :], h[:, t, :], rstd[:, t:t + 1], ln_b,
                                               ALU.mult, ALU.add).then_inc(h_ready.sem, h_ready.tick((key, t)))

                    lag = 0 if key == "ln1" else 1
                    for t in range(NT + lag + 1):
                        if t < NT:
                            moments_of(t)
                        if lag <= t < NT + lag:
                            normalise(t - lag)
                        if t > lag:
                            take_hT(key, t - lag - 1, l)

                def rope(r, key, src_key, dst, l):
                    zb = book.where.get(src_key, 0)
                    in_sbuf(zb, src_key, l)
                    V.tensor_tensor(r1, z[r % 2], cos, ALU.mult).then_inc(dve_seq.sem, dve_seq.tick())
                    b = 4 + r % 2
                    filled(b, ("rope", r), l)
                    V.tensor_tensor(r2, bank[b].t, sin, ALU.mult).then_inc(bank[b].read, 1)
                    dve.wait_ge(dve_seq.sem, dve_seq.now(l))
                    in_sbuf(b, ("rope", r), l)
                    V.tensor_tensor(dst, r1, r2, ALU.add).then_inc(roped.sem, roped.tick(("n", r)))
                    roped.marks[key] = roped.marks[("n", r)]
                    dve.wait_ge(roped.sem, roped.now(l))

                def index_scores(l):
                    m = 0
                    for t in range(1, NT):
                        W = width(t)
                        for hd in range(IDX_H):
                            in_sbuf(hd, ("logit", t, hd), l)
                            w1 = iw[:, t, hd:hd + 1]
                            if hd == 0:
                                ins = V.tensor_scalar(score[t], relu[m % 2][:, 0:W], w1, None, ALU.mult)
                            else:
                                ins = V.scalar_tensor_tensor(score[t], relu[m % 2][:, 0:W], w1, score[t], ALU.mult,
                                                             ALU.add)
                            link(ins, l, key=("weighed", m))
                            m += 1
                        link(V.tensor_tensor(score[t][:, t * P:W], score[t][:, t * P:W], chunk_mask, ALU.add), l)

                def forget_sums(l):
                    b = book.where.get("ff", 0)
                    filled(b, "ff", l)
                    dve.wait_ge(small_land.sem, small_land.at("all", l))
                    V.tensor_scalar(ffx, bank[b].t[0:8, :], b_f[:, 0:1], None, ALU.add).then_inc(bank[b].read, 1)
                    in_sbuf(b, "ff", l)
                    V.scalar_tensor_tensor(ffe, ffx, -1.0, ffx, ALU.mult, ALU.min).then_inc(
                        ffe_ready.sem, ffe_ready.tick("ffe"))
                    dve.wait_ge(ffl_ready.sem, ffl_ready.at("ffl", l))
                    link(V.scalar_tensor_tensor(ffx, ffx, 0.0, ffe, ALU.min, ALU.subtract), l)
                    link(V.memset(c_parts, 0.0), l)
                    link(V.tensor_tensor_scan(cT, zeros[0:8, 0:1].to_broadcast([8, T]), ffx, 0.0, ALU.add, ALU.add), l)
                    rest = cT
                    for part in range(3):
                        link(V.tensor_copy(c_part, rest), l)
                        if part < 2:
                            link(V.tensor_tensor(c_rest, rest, c_part, ALU.subtract), l)
                            rest = c_rest
                        V.tensor_copy(c_parts[32 * part:32 * part + 8, :], c_part).then_inc(
                            cum_ready.sem, cum_ready.tick("cum"))
                        dve.wait_ge(cum_ready.sem, cum_ready.now(l))

                def pick_keys(l, n, last):
                    for m in range(n, last):
                        t, r = 1 + m // (TOPK // 8), m % (TOPK // 8)
                        alone(dve)
                        link(V.max(top8, score[t]), l)
                        alone(dve)
                        link(V.match_replace(score[t], top8, score[t], TAKEN), l)
                        if r == TOPK // 8 - 1:
                            V.tensor_scalar(keep[:, (t - 1) * T:(t - 1) * T + width(t)], score[t], 0.5 * TAKEN, NEG,
                                            ALU.is_gt, ALU.mult).then_inc(keep_ready.sem, keep_ready.tick("keep"))

                def lambdas(l):
                    dve.wait_ge(lam_exp.sem, lam_exp.at("lam", l))
                    link(V.tensor_tensor(lamw[:, 6:7], lamw[:, 5:6], lamw[:, 4:5], ALU.subtract), l)
                    V.tensor_tensor(neg_lam, lamw[:, 6:7], laminit[:, 0:1], ALU.subtract).then_inc(
                        dve_seq.sem, dve_seq.tick())
                    link(V.tensor_scalar(norm_g[:, :], norm_g[:, :], laminit[:, 1:2], None, ALU.mult), l)

                def attention(br, l):
                    def row_max(n):
                        W = width(tile_of(n))
                        b = 2 * (n % 2)
                        filled(b, ("score", br, n, 0), l)
                        filled(b + 1, ("score", br, n, 1), l)
                        V.tensor_reduce(neg_max[n % 2], ps[:, b:b + 2, 0:W], AX.X, ALU.max, negate=True).then_inc(
                            max_ready.sem, max_ready.tick((br, n)))

                    def normalise(n):
                        W = width(tile_of(n))
                        b = 2 * (n % 2)
                        r = rcp[n % 2]
                        pb = [pbuf[:, n % 2, j, 0:W] for j in range(2)]
                        in_sbuf(b, ("score", br, n, 0), l)
                        in_sbuf(b + 1, ("score", br, n, 1), l)
                        link(V.reciprocal(r, psum_row[n % 2]), l)
                        if br == "d":
                            link(V.tensor_tensor(rcl[n % 2], r[:, 1:2], neg_lam, ALU.mult), l)
                            link(V.tensor_scalar(pb[1], pb[1], rcl[n % 2], None, ALU.mult), l)
                            V.scalar_tensor_tensor(pb[0], pb[0], r[:, 0:1], pb[1], ALU.mult, ALU.add).then_inc(
                                p_ready.sem, p_ready.tick((br, n)))
                        else:
                            for j in range(2):
                                V.tensor_scalar(pb[j], pb[j], r[:, j:j + 1], None, ALU.mult).then_inc(
                                    p_ready.sem, p_ready.tick((br, n)))

                    def take_probs(n):
                        W = width(tile_of(n))
                        filled(5, ("pt", br, n, 1), l)
                        if n >= 2:
                            filled(6 + n % 2, ("o", br, n - 2), l)
                        V.tensor_copy(ptb[:, n % 2, 512:512 + W], bank[5].t[:, 0:W]).then_inc(bank[5].read, 1)

                    def head_norm(n):
                        b = 6 + n % 2
                        dve.wait_ge(rms_ready.sem, rms_ready.at(n, l))
                        filled(b, ("o", br, n), l)
                        V.scalar_tensor_tensor(onorm[n % 2], bank[b].t[:, 0:P], rms[n % 2], norm_g[:, :], ALU.mult,
                                               ALU.mult).then_inc(bank[b].read, 1)

                    for n in range(NSTEP + 3):
                        if n < NSTEP:
                            row_max(n)
                        if 1 <= n < NSTEP + 1:
                            normalise(n - 1)
                        if br != "d" and 2 <= n < NSTEP + 2:
                            take_probs(n - 2)
                        if br == "d" and n >= 3:
                            head_norm(n - 3)

                def gated_sum(br, l):
                    if br == BRANCHES[0]:
                        dve.wait_ge(zero_land.sem, zero_land.at("all"))
                    first = unit_no[br + "g0", 0]
                    for c in range(KD):
                        b = c % 2
                        split_to(units[min(first + c + 1, len(units) - 1)], l)
                        if br == "f":
                            pick_keys(l, 24 + 3 * c, 27 + 3 * c)
                        in_sbuf(b, ("g", br, c), l)
                        filled(2 + b, ("br", br, c), l)
                        dst = yT[:, c, :] if br == BRANCHES[0] else prod
                        V.tensor_tensor(dst, gate[b], bank[2 + b].t, ALU.mult).then_inc(bank[2 + b].read, 1)
                        in_sbuf(2 + b, ("br", br, c), l)
                        if br != BRANCHES[0]:
                            V.tensor_tensor(yT[:, c, :], yT[:, c, :], prod, ALU.add).then_inc(
                                y_ready.sem, y_ready.tick("y"))
                            dve.wait_ge(y_ready.sem, y_ready.now(l))
                    split_to(units[min(first + KD + 1, len(units) - 1)], l)

                def mixer_rows(l):
                    def source(t):
                        for half in range(2):
                            b = 4 + (2 * t + half) % 4
                            filled(b, ("m", t, half), l)
                            hh = h[:, t, half * 512:(half + 1) * 512]
                            V.scalar_tensor_tensor(hh, hh, ALPHA, bank[b].t, ALU.mult, ALU.add).then_inc(
                                bank[b].read, 1)
                            in_sbuf(b, ("m", t, half), l)
                    return source

                def route(l):
                    L = lambda ins: link(ins, l)

                    def N(ins):
                        ins.then_inc(dve_seq.sem, dve_seq.tick())

                    in_sbuf(4, "router", l)
                    N(V.memset(gsc[:, :, :], NEG))
                    for t in range(NT):
                        N(V.tensor_tensor(sel[:, t, :], aff[:, t, :], br[:, :], ALU.add))
                    dve.wait_ge(dve_seq.sem, dve_seq.now(l))
                    alone(dve)
                    for g in range(NT * NGRP):
                        N(V.max(srt[:, g, :], sel.rearrange("p t e -> p (t e)")[:, g * EPG:(g + 1) * EPG]))
                    dve.wait_ge(dve_seq.sem, dve_seq.now(l))
                    L(V.tensor_tensor(gsc[:, :, 0:NGRP], srt[:, :, 0].rearrange("p (t g) -> p t g", g=NGRP),
                                      srt[:, :, 1].rearrange("p (t g) -> p t g", g=NGRP), ALU.add))
                    alone(dve)
                    for t in range(NT):
                        N(V.max(gtop[:, t, :], gsc[:, t, :]))
                    dve.wait_ge(dve_seq.sem, dve_seq.now(l))
                    alone(dve)
                    for t in range(NT):
                        N(V.max_index(gidx[:, t, :], gtop[:, t, :], gsc[:, t, :]))
                    dve.wait_ge(dve_seq.sem, dve_seq.now(l))
                    L(V.tensor_copy(gidf, gidx[:, :, 0]))
                    for t in range(NT):
                        N(V.tensor_scalar(gm[:, t, :], iota_g, gidf[:, t:t + 1], None, ALU.is_equal))
                    dve.wait_ge(dve_seq.sem, dve_seq.now(l))
                    N(V.tensor_scalar(tmp, gm, -NEG, NEG, ALU.mult, ALU.add))
                    L(V.tensor_tensor(sel, sel, gm, ALU.mult))
                    L(V.tensor_tensor(sel, sel, tmp, ALU.add))
                    alone(dve)
                    for t in range(NT):
                        N(V.max(etop[:, t, :], sel[:, t, :]))
                    dve.wait_ge(dve_seq.sem, dve_seq.now(l))
                    alone(dve)
                    for t in range(NT):
                        N(V.max_index(eidx[:, t, :], etop[:, t, :], sel[:, t, :]))
                    dve.wait_ge(dve_seq.sem, dve_seq.now(l))
                    for k in range(2):
                        N(V.tensor_copy(eidf[:, k, :], eidx[:, :, k]))
                    dve.wait_ge(dve_seq.sem, dve_seq.now(l))
                    for k in range(2):
                        for t in range(NT):
                            N(V.tensor_scalar(hot[:, k, t, :], iota_e, eidf[:, k, t:t + 1], None, ALU.is_equal))
                    dve.wait_ge(dve_seq.sem, dve_seq.now(l))
                    V.tensor_tensor(both, hot[:, 0], hot[:, 1], ALU.add).then_inc(hot_ready.sem, hot_ready.tick("hot"))
                    for k in range(2):
                        N(V.tensor_tensor((tmp, gm)[k], hot[:, k], aff, ALU.mult))
                    dve.wait_ge(dve_seq.sem, dve_seq.now(l))
                    for k in range(2):
                        N(V.tensor_reduce(wts[:, k, :], (tmp, gm)[k], AX.X, ALU.add))
                    dve.wait_ge(dve_seq.sem, dve_seq.now(l))
                    L(V.tensor_tensor(wsum[:, 0, :], wts[:, 0, :], wts[:, 1, :], ALU.add))
                    L(V.reciprocal(wsum[:, 1, :], wsum[:, 0, :]))
                    for k in range(2):
                        N(V.tensor_tensor(wts_keep[:, k, :], wts[:, k, :], wsum[:, 1, :], ALU.mult))
                    filled(5, "rank", l)
                    for k in range(2):
                        N(V.tensor_tensor((tmp, gm)[k], hot[:, k],
                                          bank[5].t[:, 0:P].rearrange("p (t e) -> p t e", e=NEXP), ALU.mult))
                    V.tensor_copy(cum, bank[5].t[:, P:P + NEXP]).then_inc(bank[5].read, 1)
                    dve.wait_ge(dve_seq.sem, dve_seq.now(l))
                    for k in range(2):
                        N(V.tensor_reduce(rank[:, k, :], (tmp, gm)[k], AX.X, ALU.add))
                    in_sbuf(5, "rank", l)
                    L(V.tensor_scalar(ovc, cum, float(C), None, ALU.is_gt))
                    L(V.tensor_scalar(quo, rank, float(C), None, ALU.is_ge))
                    N(V.tensor_copy(r8b, quo))
                    for q in range(2, OVQ + 1):
                        N(V.scalar_tensor_tensor(ovc, cum, float(q * C), ovc, ALU.is_gt, ALU.add))
                        L(V.scalar_tensor_tensor(quo, rank, float(q * C), quo, ALU.is_ge, ALU.add))
                    L(V.tensor_tensor_scan(cum, zeros[:, 0:NEXP], ovc, 0.0, ALU.add, ALU.add))
                    L(V.tensor_tensor(base, cum, ovc, ALU.subtract))
                    for k in range(2):
                        for t in range(NT):
                            N(V.tensor_tensor((tmp, gm)[k][:, t, :], hot[:, k, t, :], base, ALU.mult))
                    dve.wait_ge(dve_seq.sem, dve_seq.now(l))
                    for k in range(2):
                        N(V.tensor_reduce(bas[:, k, :], (tmp, gm)[k], AX.X, ALU.add))
                    dve.wait_ge(dve_seq.sem, dve_seq.now(l))
                    L(V.scalar_tensor_tensor(r8a, bas, float(NEXP - 1), quo, ALU.add, ALU.add))
                    L(V.tensor_tensor(r8a, r8a, eidf, ALU.subtract))
                    L(V.tensor_tensor(r8a, r8a, r8b, ALU.mult))
                    L(V.tensor_tensor(r8a, r8a, eidf, ALU.add))
                    L(V.scalar_tensor_tensor(slotf, quo, -float(C), rank, ALU.mult, ALU.add))
                    L(V.scalar_tensor_tensor(slotf, r8a, float(C), slotf, ALU.mult, ALU.add))
                    V.tensor_copy(slot_keep[:, :, :], slotf).then_inc(slot_ready.sem, slot_ready.tick("slot"))
                    for j in range(NOV):
                        N(V.tensor_scalar(ovt[:, j, :], cum[0:1, :], float(j), None, ALU.is_le))
                    dve.wait_ge(dve_seq.sem, dve_seq.now(l))
                    L(V.tensor_reduce(schedf[:, 1:1 + NOV], ovt, AX.X, ALU.add))
                    L(V.tensor_scalar(schedf[:, 1:1 + NOV], schedf[:, 1:1 + NOV], float(NEXP - 1), None, ALU.min))
                    L(V.tensor_copy(schedf[:, 0:1], cum[0:1, NEXP - 1:NEXP]))
                    V.tensor_copy(sched[:, :], schedf).then_inc(sched_ready.sem, sched_ready.tick("sched"))

                def combine(l):
                    def source(t):
                        dve.wait_ge(h_scaled.sem, h_scaled.at("h", l))
                        dve.wait_ge(got_land[t].sem, got_land[t].at(t, l))
                        link(V.scalar_tensor_tensor(h[:, t, :], got[t][0], wts_keep[:, 0, t:t + 1], h[:, t, :],
                                                    ALU.mult, ALU.add), l)
                        V.scalar_tensor_tensor(h[:, t, :], got[t][1], wts_keep[:, 1, t:t + 1], h[:, t, :],
                                               ALU.mult, ALU.add).then_inc(got_used.sem, got_used.tick(t))
                        dve.wait_ge(got_used.sem, got_used.now(l))
                    return source

                book.scope = "pre"
                dve.wait_ge(pos_land.sem, pos_land.at("all"))
                link(V.tensor_copy(z[0], r1.bitcast(I32)))
                link(V.tensor_scalar(z[0], z[0], inv_freq, None, ALU.mult))
                link(V.tensor_scalar(r2, z[0], 1 / (2 * math.pi), MAGIC, ALU.mult, ALU.add))
                link(V.tensor_scalar(r2, r2, MAGIC, None, ALU.subtract))
                for c in (C1, C2, C3):
                    link(V.scalar_tensor_tensor(z[0], r2, -c, z[0], ALU.mult, ALU.add))
                link(V.tensor_scalar(z[1], z[0], math.pi / 2, None, ALU.add))
                link(V.tensor_scalar(r2, z[1], math.pi, -2 * math.pi, ALU.is_gt, ALU.mult))
                link(V.tensor_tensor(z[1], z[1], r2, ALU.add))
                link(V.tensor_scalar(z[1], z[1], -PI_LO, PI_LO, ALU.max, ALU.min))
                V.tensor_scalar(z[0], z[0], -PI_LO, PI_LO, ALU.max, ALU.min).then_inc(
                    angle_ready.sem, angle_ready.tick("angles"))
                dve.wait_ge(x_land.sem, x_land.at("all"))
                dve.wait_ge(const_land.sem, const_land.at("all"))
                layer_norm("ln0", 0, lambda t: None)
                dve.wait_ge(wr_hi_ready.sem, wr_hi_ready.at("wr"))
                V.tensor_tensor(wr_lo[:, :, :], wr, wr_hi[:, :, :].bitcast(F32), ALU.subtract).then_inc(
                    wr_ready.sem, wr_ready.tick("wr"))
                dve.wait_ge(act_seq.sem, act_seq.at("trig"))
                link(V.tensor_scalar(sin, sin, sign_half, None, ALU.mult), key="trig")
                dve.wait_ge(pool_seq.sem, pool_seq.at("zeros"))
                count_blocks(dve)
                with dve.Fori(0, DEPTH) as l:
                    book.scope = "layer"
                    split[0] = 0
                    for r, (key, dst) in enumerate((("iq0", iqT[:, 0, :]), ("iq1", iqT[:, 1, :]), ("ik", ikT))):
                        split_to(units[r + 2], l)
                        rope(r, key, key, dst, l)
                    split_to(("fq", 1), l)
                    b_iw = book.where.get("iw", 0)
                    filled(b_iw, "iw", l)
                    V.tensor_scalar(iw[:, :, :], bank[b_iw].t[:, 0:NT * IDX_H].rearrange("p (t c) -> p t c", c=IDX_H),
                                    (IDX_H * HD) ** -0.5, None, ALU.mult).then_inc(bank[b_iw].read, 1)
                    in_sbuf(b_iw, "iw", l)
                    index_scores(l)
                    dve.wait_ge(small_land.sem, small_land.at("all", l))
                    pairs = lamv[:, :, :].rearrange("p (a b) d -> p a b d", b=2)
                    link(V.tensor_tensor(pairs[:, :, 0, :], pairs[:, :, 0, :], pairs[:, :, 1, :], ALU.mult), l)
                    V.tensor_reduce(lamw[:, 2:4], pairs[:, :, 0, :], AX.X, ALU.add).then_inc(
                        lam_prod.sem, lam_prod.tick("lam"))
                    forget_sums(l)
                    lambdas(l)
                    for m in range(12):
                        pick_keys(l, 2 * m, 2 * m + 2)
                        split_to(units[unit_no["fq", 2] + m], l)
                    r = 3
                    for br_ in BRANCHES:
                        if br_ != "f":
                            for what, dst in (("q", qT), ("k", kT)):
                                for n in range(KB):
                                    split_to(units[unit_no[br_ + what, n] + 2], l)
                                    rope(r, (br_ + what, n), (br_ + what, n), dst[:, n, :], l)
                                    r += 1
                            split_to((br_ + "g0", 1), l)
                        attention(br_, l)
                        gated_sum(br_, l)
                    layer_norm("ln1", l, mixer_rows(l))
                    route(l)

                    def rows(e, i=0):
                        n = e % 2
                        filled(1, ("x", e, 1), l, i)
                        V.tensor_copy(xT[n][:, 4:8, :], bank[1].t[:, 0:4 * C].rearrange(
                            "p (k c) -> p k c", c=C)).then_inc(bank[1].read, 1)

                    rows(0)
                    with dve.Fori(0, NTURN) as i:
                        book.scope = "pair"

                        def hidden(e):
                            n = e % 2
                            b = 3 + 2 * n
                            in_sbuf(b - 1, ("gu", e, 0), l, i)
                            filled(b, ("gu", e, 1), l, i)
                            V.tensor_tensor(hid[n], act_g[n], bank[b].t[:, 0:FE * C].rearrange(
                                "p (k c) -> p k c", c=C), ALU.mult).then_inc(bank[b].read, 1)

                        def y_half(e):
                            n = e % 2
                            filled(7, ("y", e, 1), l, i)
                            if e < 2:
                                dve.wait_ge(ysb_free[n].sem, ysb_free[n].start(l, i))
                            else:
                                dve.wait_ge(y_stored[n].sem, y_stored[n].start(l, i) + 16)
                            V.tensor_copy(ysb[n][:, 512:1024], bank[7].t[0:C, :]).then_inc(bank[7].read, 1)

                        for e in range(EPT):
                            hidden(e)
                            rows(e + 1, i)
                            y_half(e)
                    book.scope = "tail"
                    for n in range(2):
                        dve.wait_ge(y_stored[n].sem, y_stored[n].at("y", l))

                    def over_block(j, b):
                        dve.wait_ge(over_t.sem, over_t.value("over", 1, 0, b))
                        for half in range(2):
                            ins = V.tensor_copy(xT[0][:, 4 * half:4 * half + 4, :],
                                                bank[half].t[:, 0:4 * C].rearrange("p (k c) -> p k c", c=C))
                        ins.then_inc(over_xT.sem, over_xT.tick())
                        dve.wait_ge(over_act.sem, over_act.value("over", 1, 0, b))
                        V.tensor_tensor(hid[0], act_g[0], bank[3].t[:, 0:FE * C].rearrange("p (k c) -> p k c", c=C),
                                        ALU.mult).then_inc(over_h.sem, over_h.tick())
                        dve.wait_ge(over_y.sem, over_y.value("over", 1, 0, b))
                        V.tensor_copy(ysb[0][:, 0:512], bank[6].t[0:C, :])
                        V.tensor_copy(ysb[0][:, 512:1024], bank[7].t[0:C, :]).then_inc(over_ye.sem, over_ye.tick())

                    overflow(dve, l, over_block)
                    layer_norm("ln2", l, combine(l))

            @block.gpsimd
            def _(pool):
                G = nc.gpsimd

                def inverse_roots(key, l=0):
                    for t in range(NT):
                        pool.wait_ge(moments_ready.sem, moments_ready.at((key, t), l))
                        alone(pool)
                        G.tensor_scalar(lameps[:, t:t + 1], moments[:, t, 1:2], EPS, None, ALU.add).then_inc(
                            pool_seq.sem, pool_seq.tick())
                        pool.wait_ge(pool_seq.sem, pool_seq.now(l))
                        alone(pool)
                        G.tensor_tensor(rstd[:, t:t + 1], lameps[:, t:t + 1], m_half, ALU.pow).then_inc(
                            rstd_ready.sem, rstd_ready.tick((key, t)))

                def norm_params(key, g, b, l):
                    for src, dst in ((g, ln_g), (b, ln_b)):
                        pool.dma_start(dst, src[bass.ds(l, 1), :].rearrange("o c -> (o c)").partition_broadcast(P)
                                       ).then_inc(ln_land.sem, ln_land.tick(key, 16))

                def load_rows(l, n, blk, i=NTURN - 1):
                    pool.dma_start(xin[n], x_rows[blk, :]).then_inc(xin_land[n].sem, xin_land[n].tick("x", 16))

                book.scope = "pre"
                for sig in ysb_free:
                    pool.sem_inc(sig.sem, sig.tick())
                G.memset(zeros[:, :], 0.0).then_inc(pool_seq.sem, pool_seq.tick("zeros"))
                pool.wait_ge(pool_seq.sem, pool_seq.now())
                alone(pool)
                pool.wait_ge(const_land.sem, const_land.at("all"))
                alone(pool)
                inverse_roots("ln0")
                pool.wait_ge(land[RING - 1].sem, land[RING - 1].at(pieces[RING - 1]))
                alone(pool)
                G.memset(zero_row, 0.0).then_inc(pool_seq.sem, pool_seq.tick())
                pool.wait_ge(pool_seq.sem, pool_seq.now())
                for dst in (x_rows, y_rows[NEXP * C:, :]):
                    n, rest = divmod(dst.shape[0], P)
                    pool.dma_start(dst[0:n * P, :].rearrange("(n p) d -> p n d", p=P),
                                   zero_row.unsqueeze(1).to_broadcast([P, n, D])).then_inc(
                        zero_land.sem, zero_land.tick("all", 16))
                    if rest:
                        pool.dma_start(dst[n * P:, :], zero_row[0:rest, :]).then_inc(
                            zero_land.sem, zero_land.tick("all", 16))
                count_blocks(pool)
                with pool.Fori(0, DEPTH) as l:
                    book.scope = "layer"
                    for n in range(NSTEP):
                        pool.wait_ge(ssq_ready.sem, ssq_ready.at(n, l))
                        alone(pool)
                        G.tensor_scalar(rms_t[n % 2], ssq[n % 2], 1.0 / P, EPS, ALU.mult, ALU.add).then_inc(
                            pool_seq.sem, pool_seq.tick())
                        pool.wait_ge(pool_seq.sem, pool_seq.now(l))
                        alone(pool)
                        G.tensor_tensor(rms[n % 2], rms_t[n % 2], m_half, ALU.pow).then_inc(
                            rms_ready.sem, rms_ready.tick(n))
                    for n in (NSTEP - 2, NSTEP - 1):
                        b = 6 + n % 2
                        pool.wait_ge(bank[b].full.sem, bank[b].full.at(("o", "s", n), l))
                        alone(pool)
                    norm_params("ln1", ln1_g, ln1_b, l)
                    inverse_roots("ln1", l)
                    pool.wait_ge(h_ready.sem, h_ready.at(("ln1", NT - 1), l))
                    alone(pool)
                    norm_params("ln2", ln2_g, ln2_b, l)
                    pool.wait_ge(zero_land.sem, zero_land.at("all"))
                    alone(pool)
                    pool.wait_ge(slot_ready.sem, slot_ready.at("slot", l))
                    alone(pool)
                    for k in range(2):
                        for t in range(NT):
                            pool.indirect_dma_start(
                                out=x_rows, out_offset=bass.IndirectOffsetOnAxis(ap=slot_keep[:, k, t:t + 1], axis=0),
                                in_=h[:, t, :], in_offset=None).then_inc(scattered.sem, scattered.tick("all", 16))
                    pool.wait_ge(scattered.sem, scattered.at("all", l))
                    alone(pool)
                    load_rows(l, 0, slice(0, C))
                    load_rows(l, 1, slice(C, 2 * C))
                    with pool.Fori(0, NTURN) as i:
                        book.scope = "pair"
                        def next_rows(e):
                            full = bank[1].full
                            pool.wait_ge(full.sem, full.at(("x", e, 1), l, i) if e else full.start(l, i))
                            alone(pool)
                            load_rows(l, e % 2, bass.ds((i * EPT + e + 2) * C, C), i)

                        def store(e):
                            for half in range(2):
                                b = 6 + half
                                pool.wait_ge(bank[b].read, bank[b].full.at(("y", e, half), l, i))
                                alone(pool)
                            pool.dma_start(y_rows[bass.ds((i * EPT + e) * C, C), :], ysb[e % 2]).then_inc(
                                y_stored[e % 2].sem, y_stored[e % 2].tick("y", 16))

                        next_rows(0)
                        for e in range(EPT):
                            if e + 1 < EPT:
                                next_rows(e + 1)
                            store(e)
                        for n in range(2):
                            pool.wait_ge(y_stored[n].sem, y_stored[n].now(l, i))
                            pool.sem_inc(ysb_free[n].sem, ysb_free[n].tick())
                    book.scope = "tail"
                    for n in range(2):
                        pool.wait_ge(xin_land[n].sem, xin_land[n].now(l))
                        alone(pool)
                    pool.wait_ge(bank[1].full.sem, bank[1].full.at(("x", EPT, 1), l))
                    alone(pool)

                    def over_rows(j, b):
                        pool.dma_start(xin[0], x_rows[bass.ds(j * C + NEXP * C, C), :]).then_inc(
                            over_x.sem, over_x.tick(by=16))
                        pool.wait_ge(over_ye.sem, over_ye.value("over", 1, 0, b))
                        alone(pool)
                        pool.dma_start(y_rows[bass.ds(j * C + NEXP * C, C), :], ysb[0]).then_inc(
                            over_st.sem, over_st.tick(by=16))
                        pool.wait_ge(over_st.sem, over_st.value("over", 16, 0, b))
                        alone(pool)

                    overflow(pool, l, over_rows)
                    for n in range(2):
                        pool.wait_ge(y_stored[n].sem, y_stored[n].now(l))
                        alone(pool)
                    for t in range(NT):
                        for k in range(2):
                            pool.indirect_dma_start(
                                out=got[t][k], out_offset=None, in_=y_rows,
                                in_offset=bass.IndirectOffsetOnAxis(ap=slot_keep[:, k, t:t + 1], axis=0)).then_inc(
                                got_land[t].sem, got_land[t].tick(t, 16))
                    inverse_roots("ln2", l)
                book.scope = "post"
                for t in range(NT):
                    pool.wait_ge(h_ready.sem, h_ready.at(("ln2", t), DEPTH - 1))
                    alone(pool)
                    pool.dma_start(out[0, tok(t), :], h[:, t, :]).then_inc(out_land.sem, out_land.tick(by=16))
                pool.wait_ge(out_land.sem, out_land.now())
                alone(pool)


_INS = ['x', 'positions', 'ln_in_g', 'ln_in_b', 'w_in', 'b_forget', 'diff_lam', 'diff_norm_g', 'w_br', 'w_o', 'ln1_g',
        'ln1_b', 'w_router', 'b_router', 'w_gate', 'w_up', 'w_down', 'ln2_g', 'ln2_b']


def constants():
    i = np.arange(P)
    swap = np.zeros((P, P), np.float32)
    swap[i ^ 32, i] = 1.0
    tri = (i[:, None] < i[None, :]).astype(np.float32)
    e = np.tile(np.arange(NEXP, dtype=np.float32), (P, 1))
    freq = np.float32(10000.0) ** (-np.arange(0, HD, 2, dtype=np.float32) / np.float32(HD))
    inv = freq[i % 32][:, None].astype(np.float32)
    sign = np.where(i % HD < 32, -1.0, 1.0)[:, None].astype(np.float32)
    pick = np.zeros((P, 8), np.float32)
    for part in range(3):
        pick[32 * part + np.arange(8), np.arange(8)] = -1.0
    cf = np.concatenate([np.eye(P, dtype=np.float32), swap, e,
                         np.floor(e / EPG), inv, sign, np.full((P, 1), -0.5, np.float32)], 1)
    chunk = np.where(i[None, :] < (i[:, None] // CHUNK + 1) * CHUNK, 0.0, NEG)
    causal = np.where(i[None, :] <= i[:, None], 0.0, NEG)
    cb = np.concatenate([np.eye(P), chunk, causal, tri, np.ones((P, P)), pick], 1).astype(mybir.dt.np(BF16))
    lam = [0.8 - 0.6 * math.exp(-0.3 * l) for l in range(DEPTH)]
    cl = np.array([[a, 1.0 - a] for a in lam], np.float32)
    return dict(c_f32=np.ascontiguousarray(cf, np.float32), c_bf16=cb, c_lam=cl)


def kernel(**inputs):
    import concourse.bacc as bacc
    from concourse.bass_utils import run_bass_kernel_spmd as run

    arrays = {f"in_{k}": np.ascontiguousarray(inputs[k]) for k in _INS}
    arrays |= constants()
    book = Book()
    while True:
        nc = bacc.Bacc("TRN2", target_bir_lowering=False, num_devices=1)
        args = [nc.dram_tensor(k, a.shape, mybir.dt.from_np(a.dtype), kind="ExternalInput").ap()
                for k, a in arrays.items()]
        out = nc.dram_tensor("out", (1, T, D), F32, kind="ExternalOutput").ap()
        trunk(nc, book, args, out)
        if book.close():
            break
    r = run(nc, [arrays], core_ids=[0])
    return r.results[0]["out"]
```
